# Optimizing a Trainium2 kernel written in Bass

```python
import jax, jax.numpy as jnp
from jax import lax
import numpy as np

D_MODEL = 1024
BATCH = 1
SEQ = 1024
DEPTH = 2

GRID_W = 64
CTX_LEN = 256
HEAD_DIM = 64
HALF_ROT = HEAD_DIM // 2
AXIS_FREQS = HEAD_DIM // 4
ROPE_THETA = 10000.0
RW_HEADS = 6
RW_DIM = RW_HEADS * HEAD_DIM
RW_LORA_W = 64
RW_LORA_A = 64
AT_HEADS = 6
AT_KV_HEADS = 2
AT_GROUP = AT_HEADS // AT_KV_HEADS
AT_DIM = AT_HEADS * HEAD_DIM
AT_KV_DIM = AT_KV_HEADS * HEAD_DIM
WINDOW = 128
BLOCK = 128
CV_GROUPS = 4
CV_DIM = CV_GROUPS * HEAD_DIM
CONV_W = 3
D_MIX = RW_DIM + AT_DIM + CV_DIM
IN_SPLITS = (RW_DIM, RW_DIM, RW_DIM, RW_DIM, 2 * RW_LORA_W, 2 * RW_LORA_A,
             AT_DIM, AT_KV_DIM, AT_KV_DIM, AT_DIM,
             CV_DIM, CV_DIM, CV_DIM, CV_DIM)
D_IN = 4 * RW_DIM + 2 * RW_LORA_W + 2 * RW_LORA_A + 2 * AT_DIM + 2 * AT_KV_DIM + 4 * CV_DIM
NORM_EPS = 1e-6
LNX_EPS = 64e-5
MASK_VALUE = -1e30

kernel_name = "hybrid_rwkv7_swa_shortconv_dit"

def rmsnorm(x, g):
    xf = x.astype(jnp.float32)
    y = xf * lax.rsqrt(jnp.mean(xf * xf, axis=-1, keepdims=True) + NORM_EPS)
    return (y * g.astype(jnp.float32)).astype(x.dtype)

def to_heads(t):
    return t.reshape(t.shape[:-1] + (-1, HEAD_DIM))

def axial_rope_tables(row, col):
    inv = ROPE_THETA ** (-jnp.arange(AXIS_FREQS, dtype=jnp.float32) / AXIS_FREQS)
    ang = jnp.concatenate([row.astype(jnp.float32)[:, None] * inv,
                           col.astype(jnp.float32)[:, None] * inv], axis=-1)
    return jnp.cos(ang), jnp.sin(ang)

def apply_rope(t, cos, sin):
    tf = t.astype(jnp.float32)
    t1, t2 = tf[..., :HALF_ROT], tf[..., HALF_ROT:]
    c, s = cos[:, None, :], sin[:, None, :]
    return jnp.concatenate([t1 * c - t2 * s, t1 * s + t2 * c], axis=-1).astype(t.dtype)

def rwkv7_scan(r, w, k, v, kk, a, s0, reverse):
    def step(S, inp):
        r_t, w_t, k_t, v_t, kk_t, a_t = inp
        sa = jnp.einsum("bhvk,bhk->bhv", S, kk_t)
        S = (S * w_t[:, :, None, :] - sa[..., None] * (kk_t * a_t)[:, :, None, :]
             + v_t[..., None] * k_t[:, :, None, :])
        return S, jnp.einsum("bhvk,bhk->bhv", S, r_t)
    xs = tuple(jnp.moveaxis(t.astype(jnp.float32), 1, 0) for t in (r, w, k, v, kk, a))
    s_final, ys = lax.scan(step, s0, xs, reverse=reverse)
    return jnp.moveaxis(ys, 0, 1), s_final

def rwkv7_branch(parts, w0, w_up, a0, a_up, k_k, k_a, r_k, ln_g, ln_b, s0):
    r, k, v, g, wd, ad = parts
    r, k, v = to_heads(r), to_heads(k), to_heads(v)
    kk = (k * k_k.reshape(RW_HEADS, HEAD_DIM)).astype(jnp.float32)
    kk = kk * lax.rsqrt(jnp.maximum(jnp.sum(kk * kk, axis=-1, keepdims=True), 1e-12))
    ys, states = [], []
    for d in range(2):
        lw = (w0[d] + jnp.tanh(wd[..., d * RW_LORA_W:(d + 1) * RW_LORA_W]) @ w_up[d]).astype(jnp.float32)
        decay = jnp.exp(-jnp.exp(-jax.nn.softplus(-lw) - 0.5))
        a = to_heads(jax.nn.sigmoid(a0[d] + ad[..., d * RW_LORA_A:(d + 1) * RW_LORA_A] @ a_up[d]))
        k_d = k * (1 + (a - 1) * k_a.reshape(RW_HEADS, HEAD_DIM))
        y_d, s_d = rwkv7_scan(r, to_heads(decay), k_d, v, kk, a, s0[d], reverse=(d == 1))
        ys.append(y_d)
        states.append(s_d)
    y = ys[0] + ys[1]
    mu = jnp.mean(y, axis=-1, keepdims=True)
    var = jnp.mean(jnp.square(y - mu), axis=-1, keepdims=True)
    y = ((y - mu) * lax.rsqrt(var + LNX_EPS) * ln_g.reshape(RW_HEADS, HEAD_DIM).astype(jnp.float32)
         + ln_b.reshape(RW_HEADS, HEAD_DIM).astype(jnp.float32))
    bonus = jnp.sum((r * k * r_k).astype(jnp.float32), axis=-1, keepdims=True) * v.astype(jnp.float32)
    y = (y + bonus).reshape(y.shape[:2] + (RW_DIM,)).astype(g.dtype) * jax.nn.silu(g)
    return y, (states[0], states[1])

def sink_softmax(logits, sink):
    s = jnp.broadcast_to(sink.astype(jnp.float32).reshape(AT_KV_HEADS, AT_GROUP, 1, 1),
                         logits.shape[:-1] + (1,))
    return jax.nn.softmax(jnp.concatenate([logits, s], axis=-1), axis=-1)[..., :-1]

def context_attention(qc, kc, vc, sink):
    b, n = qc.shape[:2]
    qg = qc.reshape(b, n, AT_KV_HEADS, AT_GROUP, HEAD_DIM)
    s = jnp.einsum("bqhgd,bkhd->bhgqk", qg, kc).astype(jnp.float32) * HEAD_DIM ** -0.5
    p = sink_softmax(s, sink).astype(vc.dtype)
    return jnp.einsum("bhgqk,bkhd->bqhgd", p, vc).reshape(b, n, AT_DIM)

def window_attention(q, k, v, kc, vc, sink):
    b, L = q.shape[:2]
    nb = L // BLOCK
    qb = q.reshape(b, nb, BLOCK, AT_KV_HEADS, AT_GROUP, HEAD_DIM)
    pad = ((0, 0), (BLOCK, BLOCK), (0, 0), (0, 0))
    kp = jnp.pad(k, pad).reshape(b, nb + 2, BLOCK, AT_KV_HEADS, HEAD_DIM)
    vp = jnp.pad(v, pad).reshape(b, nb + 2, BLOCK, AT_KV_HEADS, HEAD_DIM)
    kw = jnp.concatenate([kp[:, :-2], kp[:, 1:-1], kp[:, 2:]], axis=2)
    vw = jnp.concatenate([vp[:, :-2], vp[:, 1:-1], vp[:, 2:]], axis=2)
    scale = HEAD_DIM ** -0.5
    s_loc = jnp.einsum("bnqhgd,bnkhd->bnhgqk", qb, kw).astype(jnp.float32) * scale
    qpos = jnp.arange(nb)[:, None] * BLOCK + jnp.arange(BLOCK)[None, :]
    kpos = jnp.arange(nb)[:, None] * BLOCK - BLOCK + jnp.arange(3 * BLOCK)[None, :]
    valid = ((jnp.abs(qpos[:, :, None] - kpos[:, None, :]) <= WINDOW)
             & (kpos[:, None, :] >= 0) & (kpos[:, None, :] < L))
    s_loc = jnp.where(valid[None, :, None, None], s_loc, MASK_VALUE)
    s_ctx = jnp.einsum("bnqhgd,bkhd->bnhgqk", qb, kc).astype(jnp.float32) * scale
    p = sink_softmax(jnp.concatenate([s_loc, s_ctx], axis=-1), sink).astype(v.dtype)
    o = (jnp.einsum("bnhgqk,bnkhd->bnqhgd", p[..., :3 * BLOCK], vw)
         + jnp.einsum("bnhgqk,bkhd->bnqhgd", p[..., 3 * BLOCK:], vc))
    return o.reshape(b, L, AT_DIM)

def short_conv_branch(parts, cv_w):
    bg, cg, xin, g = parts
    u = jnp.pad(cg * xin, ((0, 0), (1, 1), (0, 0)))
    conv = u[:, :-2] * cv_w[0] + u[:, 1:-1] * cv_w[1] + u[:, 2:] * cv_w[2]
    return bg * conv * jax.nn.silu(g)

def hybrid_layer(x, xc, c, c_ctx, w_ada, b_ada, norm_g, w_in, w_out, rw_w0, rw_w_up, rw_a0,
                 rw_a_up, rw_k_k, rw_k_a, rw_r_k, rw_ln_g, rw_ln_b, at_sink, cv_w, cos, sin,
                 update_ctx):
    shift, scale, gate = jnp.split((jax.nn.silu(c) @ w_ada + b_ada)[:, None, :], 3, axis=-1)
    shift_c, scale_c, gate_c = jnp.split(jax.nn.silu(c_ctx) @ w_ada + b_ada, 3, axis=-1)
    h = rmsnorm(x, norm_g) * (1 + scale) + shift
    hc = rmsnorm(xc, norm_g) * (1 + scale_c) + shift_c
    offs = [int(o) for o in np.cumsum(IN_SPLITS)[:-1]]
    P = jnp.split(h @ w_in, offs, axis=-1)
    Pc = jnp.split(hc @ w_in, offs, axis=-1)
    rw_params = (rw_w0, rw_w_up, rw_a0, rw_a_up, rw_k_k, rw_k_a, rw_r_k, rw_ln_g, rw_ln_b)
    zeros = jnp.zeros((x.shape[0], RW_HEADS, HEAD_DIM, HEAD_DIM), jnp.float32)
    y_rw_c, s_ctx = rwkv7_branch(Pc[:6], *rw_params, (zeros, zeros))
    y_rw, _ = rwkv7_branch(P[:6], *rw_params, s_ctx)
    q = apply_rope(to_heads(P[6]), cos, sin)
    k = apply_rope(to_heads(P[7]), cos, sin)
    v = to_heads(P[8])
    qc, kc, vc = to_heads(Pc[6]), to_heads(Pc[7]), to_heads(Pc[8])
    y_at = window_attention(q, k, v, kc, vc, at_sink) * jax.nn.silu(P[9])
    y_cv = short_conv_branch(P[10:14], cv_w)
    x = x + gate * (jnp.concatenate([y_rw, y_at, y_cv], axis=-1) @ w_out)
    if update_ctx:
        y_at_c = context_attention(qc, kc, vc, at_sink) * jax.nn.silu(Pc[9])
        y_cv_c = short_conv_branch(Pc[10:14], cv_w)
        xc = xc + gate_c * (jnp.concatenate([y_rw_c, y_at_c, y_cv_c], axis=-1) @ w_out)
    return x, xc

def setup_inputs(seed: int = 0) -> dict:
    key = jax.random.key(seed)
    ks = jax.random.split(key, 24)
    f32 = jnp.float32
    n = jax.random.normal
    return {
        "x": n(ks[0], (BATCH, SEQ, D_MODEL), f32),
        "c": n(ks[1], (BATCH, D_MODEL), f32),
        "ctx": n(ks[2], (BATCH, CTX_LEN, D_MODEL), f32),
        "c_ctx": n(ks[3], (D_MODEL,), f32),
        "w_ada": n(ks[4], (DEPTH, D_MODEL, 3 * D_MODEL), f32) * (0.5 * D_MODEL ** -0.5),
        "b_ada": 0.02 * n(ks[5], (DEPTH, 3 * D_MODEL), f32),
        "norm_g": 1.0 + 0.02 * n(ks[6], (DEPTH, D_MODEL), f32),
        "w_in": n(ks[7], (DEPTH, D_MODEL, D_IN), f32) * D_MODEL ** -0.5,
        "w_out": n(ks[8], (DEPTH, D_MIX, D_MODEL), f32) * D_MIX ** -0.5,
        "rw_w0": jax.random.uniform(ks[9], (DEPTH, 2, RW_DIM), f32, -6.0, -1.0),
        "rw_w_up": n(ks[10], (DEPTH, 2, RW_LORA_W, RW_DIM), f32) * (0.5 * RW_LORA_W ** -0.5),
        "rw_a0": 0.1 * n(ks[11], (DEPTH, 2, RW_DIM), f32),
        "rw_a_up": n(ks[12], (DEPTH, 2, RW_LORA_A, RW_DIM), f32) * RW_LORA_A ** -0.5,
        "rw_k_k": 0.85 + 0.02 * n(ks[13], (DEPTH, RW_DIM), f32),
        "rw_k_a": 1.0 + 0.02 * n(ks[14], (DEPTH, RW_DIM), f32),
        "rw_r_k": 0.1 * n(ks[15], (DEPTH, RW_HEADS, HEAD_DIM), f32),
        "rw_ln_g": 1.0 + 0.02 * n(ks[16], (DEPTH, RW_DIM), f32),
        "rw_ln_b": 0.02 * n(ks[17], (DEPTH, RW_DIM), f32),
        "at_sink": 0.5 * n(ks[18], (DEPTH, AT_HEADS), f32),
        "cv_w": n(ks[19], (DEPTH, CONV_W, CV_DIM), f32) * CONV_W ** -0.5,
        "final_g": 1.0 + 0.02 * n(ks[20], (D_MODEL,), f32),
    }

def reference(x, c, ctx, c_ctx, w_ada, b_ada, norm_g, w_in, w_out, rw_w0, rw_w_up, rw_a0,
              rw_a_up, rw_k_k, rw_k_a, rw_r_k, rw_ln_g, rw_ln_b, at_sink, cv_w, final_g):
    L = x.shape[1]
    ROWS = L // GRID_W
    row = jnp.repeat(jnp.arange(ROWS), GRID_W)
    col = jnp.tile(jnp.arange(GRID_W), ROWS)
    cos, sin = axial_rope_tables(row, col)
    xc = ctx
    for l in range(DEPTH):
        x, xc = hybrid_layer(x, xc, c, c_ctx, w_ada[l], b_ada[l], norm_g[l], w_in[l], w_out[l],
                             rw_w0[l], rw_w_up[l], rw_a0[l], rw_a_up[l], rw_k_k[l], rw_k_a[l],
                             rw_r_k[l], rw_ln_g[l], rw_ln_b[l], at_sink[l], cv_w[l], cos, sin,
                             update_ctx=(l < DEPTH - 1))
    return rmsnorm(x, final_g)


_drawn_inputs = setup_inputs


def setup_inputs(seed=0):
    import zlib

    import numpy as np

    out = dict(_drawn_inputs(seed))
    spreads = {}
    factors = {'norm_g': 4.561,
     'rw_w_up': 8.0,
     'rw_a0': 8.0,
     'rw_k_k': 200.0,
     'rw_k_a': 195.206,
     'rw_ln_g': 200.0,
     'rw_ln_b': 200.0,
     'at_sink': 8.0,
     'final_g': 27.894}
    for name, (base, spread) in spreads.items():
        noise = np.random.default_rng([zlib.crc32(name.encode()), seed]).standard_normal(out[name].shape)
        drawn = base * np.exp(spread * noise) if base else spread * noise
        out[name] = __import__('jax').numpy.asarray(drawn.astype(out[name].dtype))
    for name, factor in factors.items():
        out[name] = (out[name] * factor).astype(out[name].dtype)
    return out
```

```python
from contextlib import ExitStack

import numpy as np

import concourse.bass as bass
from concourse import mybir

F32 = mybir.dt.float32
ALU = mybir.AluOpType
ACT = mybir.ActivationFunctionType
AX = mybir.AxisListType
ENGINE = mybir.EngineType

P = 128
DM = 1024
KT = DM // P
CTX, SEQ = 256, 1024
T = CTX + SEQ
DEPTH = 2
HD = 64
RW = 384
PAIRS = RW // P
HEADS = RW // HD
CV = 256
CVT = CV // P
CHUNK = 64
NCH = T // CHUNK
WIN = 128
NT = T // P
QB = SEQ // P
DECAY = float(np.exp(np.float32(-0.5))) / 2
NORM_EPS, LNX_EPS = 1e-6, 64e-5
MASK_VALUE = -1e30
LEVELS = (2, 4, 8, 16, 32)

N1, N2 = 15, 11
T_CG, T_XIN, T_BG, T_CGATE, T_Q, T_AGATE, T_K, T_KPAD = 0, 2, 4, 6, 8, 11, 14, 15
T_R, T_RK, T_WD, T_AD, T_G = 0, 3, 6, 7, 8
GROUPS = ((0, CTX), (CTX, CTX + 512), (CTX + 512, T))


def table(parts):
    out, at = {}, 0
    for name, n in parts:
        out[name] = at
        at += n
    return out, at


CONST, NCONST = table([
    ("ident", P), ("rot", P), ("headsum", P), ("ones", P), ("headsel", 2), ("reset", 256),
    ("id64", HD), ("maskB0", 2 * HD), ("maskK0", 2 * HD), ("maskN0", HD),
    ("maskB1", 2 * HD), ("maskK1", 2 * HD), ("maskN1", HD), ("join1", HD), ("join", 5 * HD)])
PARAM, NPARAM = table([
    ("norm_g", KT), ("w0", 2 * PAIRS), ("a0", 2 * PAIRS), ("k_k", PAIRS), ("k_a", PAIRS), ("r_k", PAIRS),
    ("cv_w", 3 * CVT), ("sink", HEADS), ("b_ada", 24)])
DERIV, NDERIV = table([("gs", 2 * KT), ("nsink", HEADS), ("hw0", 2 * PAIRS), ("ha0", 2 * PAIRS), ("hk_a", PAIRS)])


class Signal:

    def __init__(self, ctx, nc, name):
        self.sem, self.base = ctx.enter_context(nc.semaphore(name)), 0

    def at(self, k):
        return k + self.base

    def close(self, total):
        self.base += total


class Order:

    def __init__(self, eng, count):
        self.eng, self.count, self.n, self.off = eng, count, 0, 0

    def __call__(self, ins):
        ins.then_inc(self.count.sem, 1)
        self.n += 1
        return self.n

    def wait(self, n=None):
        self.eng.wait_ge(self.count.sem, (self.n if n is None else n) + self.off + self.count.base)

    def link(self, ins):
        self(ins)
        self.wait()


def build(nc, d):
    with ExitStack() as ctx:
        g = Kernel(nc, ctx, d)
        g.setup()
        for layer in range(DEPTH):
            g.norm(layer)
            g.project_first(layer)
            g.attention(layer)
            g.project_second(layer)
            for way in (0, 1):
                g.decays(layer, way)
                g.scan(layer, way)
            g.readout(layer)
            g.project_out(layer)
        g.final_norm()


class Kernel:
    def __init__(self, nc, ctx, d):
        self.nc, self.ctx, self.d = nc, ctx, d
        self.signals = {}
        self.const = ctx.enter_context(nc.sbuf_tensor("const", [P, NCONST], F32))
        self.param = ctx.enter_context(nc.sbuf_tensor("param", [P, DEPTH, NPARAM], F32))
        self.deriv = ctx.enter_context(nc.sbuf_tensor("deriv", [P, DEPTH, NDERIV], F32))
        self.ada = ctx.enter_context(nc.sbuf_tensor("ada", [P, DEPTH, 24, 2], F32))
        self.fing = ctx.enter_context(nc.sbuf_tensor("fing", [P, KT], F32))
        self.eps = ctx.enter_context(nc.sbuf_tensor("eps", [P, 2], F32))
        self.tiles = ctx.enter_context(nc.sbuf_tensor("tiles", [P, 16, T], F32))
        self.hid = ctx.enter_context(nc.sbuf_tensor("hid", [P, KT * T], F32))
        self.NEX = 18800
        self.extra = ctx.enter_context(nc.sbuf_tensor("extra", [P, self.NEX], F32))
        self.bank = [ctx.enter_context(nc.psum_tensor(f"bank{i}", [P, 512], F32)) for i in range(8)]

    def sig(self, name):
        if name not in self.signals:
            self.signals[name] = Signal(self.ctx, self.nc, name)
        return self.signals[name]

    def c(self, name, n):
        return self.const[:, CONST[name]:CONST[name] + n]

    def pr(self, layer, name, n, at=0):
        return self.param[:, layer, PARAM[name] + at:PARAM[name] + at + n]

    def dv(self, layer, name, n, at=0):
        return self.deriv[:, layer, DERIV[name] + at:DERIV[name] + at + n]

    def loop(self, engine, start, end):
        return self.nc.Fori(start, end, engines=(engine,))

    @property
    def hT(self):
        return self.hid[:, :].rearrange("p (k t) -> p k t", k=KT)

    def ex(self, at, n):
        assert at + n <= self.NEX
        return self.extra[:, at:at + n]

    def setup(self):
        nc, d = self.nc, self.d
        loads, ada_ready, ada_out, silu, small = (
            self.sig(n) for n in ("loads", "ada_ready", "ada_out", "silu", "order_dve"))
        ada_in = [self.sig(f"w_in{s}") for s in range(2)]
        cc = self.ex(0, 2 * KT).rearrange("p (k s) -> p k s", s=2)
        sc = self.ex(16, 2 * KT).rearrange("p (k s) -> p k s", s=2)
        COLS = 512
        NC_ = DEPTH * 3 * DM // COLS
        ring = [self.ex(64 + s * KT * COLS, KT * COLS).rearrange("p (k n) -> p k n", k=KT) for s in range(2)]
        acc = [self.bank[s][:, 0:8].rearrange("p (n s) -> p n s", s=2) for s in range(2)]
        raw = self.ada[:, :, :, :].rearrange("p l n s -> p (l n) s")
        with nc.Block() as block:
            @block.sync
            def _(sp):
                for dst, src in ((self.const[:, :], d["const"]), (self.param[:, :, :], d["param"]),
                                 (self.fing[:, :], d["fing"]), (cc, d["cc"])):
                    sp.dma_start(dst, src).then_inc(loads.sem, 16)
                sp.dma_start(self.tiles[:, 0:KT, :], d["x"]).then_inc(loads.sem, 16)
                for t in range(2):
                    sp.dma_start(ring[t], d["w_ada"][t]).then_inc(ada_in[t].sem, 16)
                with self.loop(ENGINE.SP, 1, NC_ // 2) as i:
                    for s in range(2):
                        sp.wait_ge(ada_ready.sem, 2 * i + s - 1)
                        sp.dma_start(ring[s], d["w_ada"][bass.ds(2 * i + s, 1)].rearrange("a p k n -> (a p) k n")
                                     ).then_inc(ada_in[s].sem, 16)

            @block.scalar
            def _(act):
                act.wait_ge(loads.sem, 80)
                act.activation(sc, cc, ACT.Silu).then_inc(silu.sem, 1)

            @block.tensor
            def _(pe):
                pe.wait_ge(silu.sem, 1)

                def tile(s, i, t, first):
                    pe.wait_ge(ada_in[s].sem, 16 * i + 16)
                    if not first:
                        pe.wait_ge(ada_out.sem, t - 1)
                    for n in range(4):
                        for k in range(KT):
                            ins = pe.matmul(acc[s][:, n, :], ring[s][:, k, n * P:(n + 1) * P], sc[:, k, :],
                                            start=(k == 0), stop=(k == KT - 1))
                    ins.then_inc(ada_ready.sem, 1)
                for s in range(2):
                    tile(s, 0, s, True)
                with self.loop(ENGINE.PE, 1, NC_ // 2) as i:
                    for s in range(2):
                        tile(s, i, 2 * i + s, False)

            @block.vector
            def _(dve):
                o = Order(dve, small)
                dve.wait_ge(loads.sem, 80)
                o(dve.memset(self.eps[:, 0:1], NORM_EPS))
                o(dve.memset(self.eps[:, 1:2], LNX_EPS))
                with self.loop(ENGINE.DVE, 0, NC_ // 2) as i:
                    for s in range(2):
                        dve.wait_ge(ada_ready.sem, 2 * i + s + 1)
                        dve.tensor_copy(raw[:, bass.ds(8 * i + 4 * s, 4), :], acc[s]).then_inc(ada_out.sem, 1)
                dve.wait_ge(ada_out.sem, NC_)
                for l in range(DEPTH):
                    b = self.pr(l, "b_ada", 24).unsqueeze(2).to_broadcast([P, 24, 2])
                    o(dve.tensor_tensor(self.ada[:, l], self.ada[:, l], b, ALU.add))
                    o(dve.tensor_scalar(self.dv(l, "nsink", HEADS), self.pr(l, "sink", HEADS), -1.0, None, ALU.mult))
                    o(dve.tensor_scalar(self.dv(l, "hw0", 6), self.pr(l, "w0", 6), 0.5, None, ALU.mult))
                    o(dve.tensor_scalar(self.dv(l, "ha0", 6), self.pr(l, "a0", 6), 0.5, None, ALU.mult))
                    o(dve.tensor_scalar(self.dv(l, "hk_a", 3), self.pr(l, "k_a", 3), 0.5, None, ALU.mult))
                    o.wait()
                    gs = self.dv(l, "gs", 2 * KT).rearrange("p (k s) -> p k s", s=2)
                    ng = self.pr(l, "norm_g", KT).unsqueeze(2).to_broadcast([P, KT, 2])
                    o.link(dve.scalar_tensor_tensor(out=gs, in0=self.ada[:, l, KT:2 * KT, :], scalar=1.0, in1=ng,
                                                    op0=ALU.add, op1=ALU.mult))
                self.total_order = o.n
        small.close(self.total_order)
        loads.close(80)
        for x in ada_in:
            x.close(8 * NC_)
        ada_ready.close(NC_), ada_out.close(NC_), silu.close(1)

    def inv_rms(self, block, x, sq, rstd, lo, groups):
        squares, sums, roots, order = (self.sig(n) for n in ("squares", "sums", "roots", "order_dve"))

        @block.scalar
        def _(act):
            for k in range(KT):
                if k >= 2:
                    act.wait_ge(sums.sem, sums.at(k - 1))
                act.activation(sq[:, k % 2, lo:T], x[:, k, lo:T], ACT.Square).then_inc(squares.sem, 1)
            for n, (a, b) in enumerate(groups):
                act.wait_ge(sums.sem, sums.at(KT))
                act.activation(rstd[:, a:b], self.bank[n][:, 0:b - a], ACT.Sqrt, scale=1.0 / DM,
                               bias=self.eps[:, 0:1]).then_inc(roots.sem, 1)

        @block.tensor
        def _(pe):
            for k in range(KT):
                pe.wait_ge(squares.sem, squares.at(k + 1))
                for n, (a, b) in enumerate(groups):
                    ins = pe.matmul(self.bank[n][:, 0:b - a], self.c("ones", P), sq[:, k % 2, a:b],
                                    start=(k == 0), stop=(k == KT - 1))
                ins.then_inc(sums.sem, 1)

    def norm(self, layer):
        nc = self.nc
        sq = self.ex(0, 2 * T).rearrange("p (s t) -> p s t", s=2)
        rstd = self.ex(2 * T, T)
        h, x = self.hT, self.tiles[:, 0:KT, :]
        roots, order = self.sig("roots"), self.sig("order_dve")
        gs = self.dv(layer, "gs", 2 * KT).rearrange("p (k s) -> p k s", s=2)
        with nc.Block() as block:
            self.inv_rms(block, x, sq, rstd, 0, GROUPS)

            @block.vector
            def _(dve):
                o = Order(dve, order)
                for n, (a, b) in enumerate(GROUPS):
                    dve.wait_ge(roots.sem, roots.at(n + 1))
                    o(dve.reciprocal(rstd[:, a:b], rstd[:, a:b]))
                o.wait()
                for k in range(KT):
                    first = o(dve.tensor_tensor(h[:, k, :], x[:, k, :], rstd, ALU.mult))
                    o.wait()
                    for s, (a, b) in ((1, (0, CTX)), (0, (CTX, T))):
                        o(dve.tensor_scalar(h[:, k, a:b], h[:, k, a:b], gs[:, k, s:s + 1],
                                            self.ada[:, layer, k, s:s + 1], ALU.mult, ALU.add))
                self.total_order = o.n
        self.sig("squares").close(KT), self.sig("sums").close(KT), roots.close(len(GROUPS))
        order.close(self.total_order)

    def stream_sync(self, sp, w, n, ring, ng):
        w_in, ready = [self.sig(f"w_in{s}") for s in range(2)], self.sig("acc_ready")

        def load(s, t):
            sp.dma_start(ring[s], w[bass.ds(t, 1)].rearrange("a p k n -> (a p) k n")).then_inc(w_in[s].sem, 16)
        for s in range(2):
            load(s, s)
        with self.loop(ENGINE.SP, 1, n // 2) as i:
            for s in range(2):
                sp.wait_ge(ready.sem, ng * (2 * i + s - 1) + ready.base)
                load(s, 2 * i + s)
        if n % 2:
            sp.wait_ge(ready.sem, ready.at(ng * (n - 2)))
            load(0, n - 1)

    def stream_pe(self, pe, rhs, n, ring, groups, last_groups):
        ready, free = self.sig("acc_ready"), self.sig("acc_free")
        w_in = [self.sig(f"w_in{s}") for s in range(2)]
        ng = len(groups)

        def tile(s, i, gs, skip):
            t = 2 * i + s
            pe.wait_ge(w_in[s].sem, 16 * i + 16 + w_in[s].base)
            for q, (a, b) in enumerate(gs):
                if not skip:
                    pe.wait_ge(free.sem, ng * t + (q + 1 - 2 * ng) + free.base)
                for k in range(KT):
                    ins = pe.matmul(self.bank[3 * s + q][:, 0:b - a], ring[s][:, k, :], rhs[:, k, a:b],
                                    start=(k == 0), stop=(k == KT - 1))
                ins.then_inc(ready.sem, 1)
        for s in range(2):
            tile(s, 0, groups, True)
        with self.loop(ENGINE.PE, 1, n // 2) as i:
            for s in range(2):
                tile(s, i, groups, False)
        if n % 2:
            pe.wait_ge(free.sem, free.at(ng * (n - 1)))
            tile(0, n // 2, last_groups, True)

    def stream_act(self, act, out, n, groups, last_groups, func=ACT.Copy):
        ready, free = self.sig("acc_ready"), self.sig("acc_free")
        ng = len(groups)

        def tile(s, t, gs):
            for q, (a, b) in enumerate(gs):
                act.wait_ge(ready.sem, ng * t + q + 1 + ready.base)
                act.activation(out[:, bass.ds(t, 1), a:b], self.bank[3 * s + q][:, 0:b - a].unsqueeze(1),
                               func).then_inc(free.sem, 1)
        with self.loop(ENGINE.Activation, 0, n // 2) as i:
            for s in range(2):
                tile(s, 2 * i + s, groups)
        if n % 2:
            tile(0, n - 1, last_groups)
        self.counts = ng * (n - n % 2) + len(last_groups) * (n % 2)

    def stream_close(self, n, total):
        self.sig("w_in0").close(16 * (n - n // 2)), self.sig("w_in1").close(16 * (n // 2))
        self.sig("acc_ready").close(total), self.sig("acc_free").close(total)

    def project_first(self, layer):
        nc, d = self.nc, self.d
        keep = layer < DEPTH - 1
        groups = GROUPS if keep else GROUPS[1:]
        lo = 0 if keep else CTX
        tiles = self.tiles
        order = self.sig("order_dve")
        free, gate, wv_in, v_ready, v_taken, v_out, trig = (
            self.sig(n) for n in ("acc_free", "gates", "wv_in", "v_ready", "v_taken", "dma_out", "trig_in"))
        rot_ready, rot_used, rope, conv_done = (self.sig(n) for n in ("rot_ready", "rot_used", "rope", "conv_done"))
        at = 0

        def take(n):
            nonlocal at
            at += n
            return self.ex(at - n, n)
        UW = T + 4
        u = take(CVT * UW).rearrange("p (i t) -> p i t", i=CVT)
        cvt = take(CVT * T).rearrange("p (i t) -> p i t", i=CVT)
        v_rw = take(NT * RW).rearrange("p (n v) -> p n v", n=NT)
        ring = [take(DM).rearrange("p (k n) -> p k n", k=KT) for _ in range(2)]
        wv = take(KT * 512).rearrange("p (k n) -> p k n", k=KT)
        assert at <= 15200
        v_at = self.v_at = self.ex(15200, (NT + 2) * P).rearrange("p (n v) -> p n v", n=NT + 2)
        trigt = self.ex(16736, 2 * SEQ).rearrange("p (s t) -> p s t", s=2)
        kpad = tiles[:, T_KPAD, :]
        rope_tiles = (T_Q, T_Q + 1, T_Q + 2, T_K)
        loops = N1 - 1
        stream = len(groups) * loops + 3
        with nc.Block() as block:
            @block.sync
            def _(sp):
                sp.dma_start(trigt, d["trig"]).then_inc(trig.sem, 16)
                sp.dma_start(wv, d["w_v"][layer]).then_inc(wv_in.sem, 16)
                self.stream_sync(sp, d["w_1"][layer], N1, ring, len(groups))
                sp.wait_ge(v_taken.sem, v_taken.at(2 * NT))
                sp.dma_start(d["v_rw"].rearrange("n p v -> p n v"), v_rw).then_inc(v_out.sem, 16)
                sp.wait_ge(conv_done.sem, conv_done.at(CVT))
                for i in range(CVT):
                    sp.dma_start(d["y"][PAIRS + i, :, lo:T], cvt[:, i, lo:T]).then_inc(v_out.sem, 16)
                sp.wait_ge(v_out.sem, v_out.at(16 + 16 * CVT))

            @block.tensor
            def _(pe):
                self.stream_pe(pe, self.hT, N1, ring, groups, GROUPS)
                pe.wait_ge(wv_in.sem, wv_in.at(16))
                for n in range(NT):
                    if n >= 2:
                        pe.wait_ge(v_taken.sem, v_taken.at(2 * n - 2))
                    for k in range(KT):
                        ins = pe.matmul(self.bank[6 + n % 2][:, :], self.hT[:, k, n * P:(n + 1) * P], wv[:, k, :],
                                        start=(k == 0), stop=(k == KT - 1))
                    ins.then_inc(v_ready.sem, 1)
                pe.wait_ge(free.sem, free.at(stream))
                pe.wait_ge(v_taken.sem, v_taken.at(2 * NT))
                for m in range(8):
                    t, (a, b) = rope_tiles[m // 2], GROUPS[1 + m % 2]
                    if m >= 2:
                        pe.wait_ge(rot_used.sem, rot_used.at(m - 1))
                    pe.matmul(self.bank[6 + m % 2][:, :], self.c("rot", P), tiles[:, t, a:b],
                              start=True, stop=True).then_inc(rot_ready.sem, 1)

            @block.scalar
            def _(act):
                self.stream_act(act, tiles, N1, groups, GROUPS)
                act.wait_ge(free.sem, free.at(stream))
                for t, n in ((T_CGATE, CVT), (T_AGATE, PAIRS)):
                    act.activation(tiles[:, t:t + n, lo:T], tiles[:, t:t + n, lo:T], ACT.Silu).then_inc(gate.sem, 1)
                for n in range(NT):
                    act.wait_ge(v_ready.sem, v_ready.at(n + 1))
                    act.copy(v_rw[:, n, :], self.bank[6 + n % 2][:, 0:RW]).then_inc(v_taken.sem, 1)
                    slot = n if n < 2 else n + 1
                    act.copy(v_at[:, slot, :], self.bank[6 + n % 2][:, RW:512]).then_inc(v_taken.sem, 1)

            @block.vector
            def _(dve):
                o = Order(dve, order)
                o(dve.memset(v_at[:, 2, :], 0.0))
                o(dve.memset(v_at[:, NT + 1, :], 0.0))
                for z in (0, CTX + 1, CTX + 2, T + 3):
                    o(dve.memset(u[:, :, z:z + 1], 0.0))
                o(dve.memset(kpad[:, 0:P], 0.0))
                o(dve.memset(kpad[:, P + SEQ:T], 0.0))
                dve.wait_ge(free.sem, free.at(4 * len(groups)))
                spans = [(0, CTX, 1), (CTX, T, 3)] if keep else [(CTX, T, 3)]
                for a, b, s in spans:
                    o(dve.tensor_tensor(u[:, :, a + s:b + s], tiles[:, T_CG:T_CG + CVT, a:b],
                                        tiles[:, T_XIN:T_XIN + CVT, a:b], ALU.mult))
                o.wait()
                w = self.pr(layer, "cv_w", 3 * CVT).rearrange("p (j i) -> p j i", j=3)
                for j in range(3):
                    for a, b, s in spans:
                        for i in range(CVT):
                            src = u[:, i, a + s + j - 1:b + s + j - 1]
                            if j == 0:
                                o(dve.tensor_scalar(cvt[:, i, a:b], src, w[:, j, i:i + 1], None, ALU.mult))
                            else:
                                o(dve.scalar_tensor_tensor(out=cvt[:, i, a:b], in0=src, scalar=w[:, j, i:i + 1],
                                                           in1=cvt[:, i, a:b], op0=ALU.mult, op1=ALU.add))
                    o.wait()
                dve.wait_ge(free.sem, free.at(6 * len(groups)))
                o.link(dve.tensor_tensor(cvt[:, :, lo:T], cvt[:, :, lo:T], tiles[:, T_BG:T_BG + CVT, lo:T], ALU.mult))
                dve.wait_ge(gate.sem, gate.at(1))
                for i in range(CVT):
                    dve.tensor_tensor(cvt[:, i, lo:T], cvt[:, i, lo:T], tiles[:, T_CGATE + i, lo:T],
                                      ALU.mult).then_inc(conv_done.sem, 1)
                dve.wait_ge(trig.sem, trig.at(16))
                for m in range(8):
                    t, (a, b) = rope_tiles[m // 2], GROUPS[1 + m % 2]
                    cos, sin = trigt[:, 0, a - CTX:b - CTX], trigt[:, 1, a - CTX:b - CTX]
                    part = u[:, m % 2, 0:512]
                    dst = tiles[:, t, a:b] if t != T_K else kpad[:, P + a - CTX:P + b - CTX]
                    dve.wait_ge(rot_ready.sem, rot_ready.at(m + 1))
                    dve.tensor_tensor(part, self.bank[6 + m % 2][:, :], sin, ALU.mult).then_inc(rot_used.sem, 1)
                    o(dve.tensor_tensor(dst, tiles[:, t, a:b], cos, ALU.mult))
                    o.wait()
                    dve.wait_ge(rot_used.sem, rot_used.at(m + 1))
                    dve.tensor_tensor(dst, dst, part, ALU.add).then_inc(rope.sem, 1)
                self.total_order = o.n
        order.close(self.total_order)
        self.stream_close(N1, stream)
        gate.close(2), wv_in.close(16), v_ready.close(NT), v_taken.close(2 * NT), v_out.close(16 + 16 * CVT)
        trig.close(16), rot_ready.close(8), rot_used.close(8), rope.close(8), conv_done.close(CVT)

    def attention(self, layer):
        nc, d = self.nc, self.d
        tiles, v_at, bank = self.tiles, self.v_at, self.bank
        strips_in, staged, scores, masked, center, nmax, probs, esink, pt, pt_d, pt_a, o_ready, o_used, inv, \
            yt_ready, yt_used = (self.sig(n) for n in (
                "strips_in", "staged", "scores", "masked", "center", "nmax", "probs", "esink", "pt", "pt_d", "pt_a",
                "o_ready", "o_used", "inv", "yt_ready", "yt_used"))
        y_out = [self.sig(f"y_out{s}") for s in range(2)]
        order = self.sig("order_dve")
        at = 0

        def take(n):
            nonlocal at
            at += n
            return self.ex(at - n, n)
        strips = take(2 * QB * P).rearrange("p (s n) -> p s n", s=2)
        qs = [take(PAIRS * P).rearrange("p (j t) -> p j t", j=PAIRS) for _ in range(2)]
        ks = [take(3 * P) for _ in range(2)]
        vs = [take(3 * P).rearrange("p (n v) -> p n v", n=3) for _ in range(2)]
        sm = [take(5 * P) for _ in range(2)]
        ptt = [take(5 * P).rearrange("p (n q) -> p n q", n=5) for _ in range(2)]
        rmax, nm, den, es, rden = (take(HEADS) for _ in range(5))
        yn = [take(RW).rearrange("p (h v) -> p h v", h=HEADS) for _ in range(2)]
        yo = [take(RW).rearrange("p (j t) -> p j t", j=PAIRS) for _ in range(2)]
        assert at <= 15200
        kpad, kctx = tiles[:, T_KPAD, :], tiles[:, T_K, 0:CTX]
        obank = bank[6][:, 0:RW].rearrange("p (h v) -> p h v", h=HEADS)
        tbank = bank[7][:, 0:RW].rearrange("p (j t) -> p j t", j=PAIRS)
        nsink, sink = self.dv(layer, "nsink", HEADS), self.pr(layer, "sink", HEADS)
        keep = layer < DEPTH - 1
        CB = CTX // P if keep else 0
        blocks = CB + QB

        def run(engine, body):
            if keep:
                for s in range(2):
                    body(s, 0, s, s, False, True)
                with self.loop(engine, 0, QB // 2) as i:
                    for s in range(2):
                        body(s, i + 1, 2 * i + s + CB, 2 * i + s, True, False)
            else:
                for s in range(2):
                    body(s, 0, s, s, True, True)
                with self.loop(engine, 1, QB // 2) as i:
                    for s in range(2):
                        body(s, i, 2 * i + s, 2 * i + s, True, False)

        def cols(b, windowed):
            return b * P + (CTX if windowed else 0)
        HP = [(n % 2, n // 2) for n in range(HEADS)]

        with nc.Block() as block:
            @block.sync
            def _(sp):
                sp.dma_start(strips, d["strips"]).then_inc(strips_in.sem, 16)

                def body(s, i, u, b, windowed, first):
                    sp.wait_ge(yt_used.sem, u + 1 + yt_used.base)
                    sp.dma_start(d["y"][0:PAIRS, :, bass.ds(cols(b, windowed), P)].rearrange("j p t -> p j t"),
                                 yo[s]).then_inc(y_out[s].sem, 16)
                run(ENGINE.SP, body)
                for x in y_out:
                    sp.wait_ge(x.sem, x.at(8 * blocks))

            @block.gpsimd
            def _(pool):
                def body(s, i, u, b, windowed, first):
                    if not first:
                        pool.wait_ge(o_ready.sem, HEADS * (u - 1) + o_ready.base)
                    pool.tensor_copy(qs[s], tiles[:, T_Q:T_Q + PAIRS, bass.ds(cols(b, windowed), P)]
                                     ).then_inc(staged.sem, 1)
                    if windowed:
                        pool.tensor_copy(ks[s], kpad[:, bass.ds(b * P, 3 * P)]).then_inc(staged.sem, 1)
                        pool.tensor_copy(vs[s], v_at[:, bass.ds(b + 2, 3), :]).then_inc(staged.sem, 1)
                    else:
                        pool.tensor_copy(ks[s][:, 0:1], kctx[:, 0:1]).then_inc(staged.sem, 1)
                        pool.tensor_copy(vs[s][:, 0, 0:1], v_at[:, 0, 0:1]).then_inc(staged.sem, 1)
                run(ENGINE.Pool, body)

            @block.tensor
            def _(pe):
                def body(s, i, u, b, windowed, first):
                    def score(n):
                        p, j = HP[n]
                        rows = slice(HD * p, HD * p + HD)
                        if n >= 2:
                            pe.wait_ge(masked.sem, HEADS * u + (n - 1) + masked.base)
                            pe.wait_ge(center.sem, 2 * (HEADS * u + (n - 1)) + center.base)
                        elif not (first and s == 0):
                            pe.wait_ge(masked.sem, HEADS * u + (n - 1) + masked.base)
                            pe.wait_ge(center.sem, 2 * (HEADS * u + (n - 1)) + center.base)
                        q = qs[s][rows, j, :]
                        if windowed:
                            pe.matmul(bank[2 * p][:, 0:3 * P], q, ks[s][rows, :], start=True, stop=True)
                        pe.matmul(bank[2 * p][:, 3 * P:4 * P], q, kctx[rows, 0:P], start=True, stop=True)
                        pe.matmul(bank[2 * p + 1][:, 0:P], q, kctx[rows, P:2 * P], start=True,
                                  stop=True).then_inc(scores.sem, 1)

                    def turn(n):
                        if n > 0 or not (first and s == 0):
                            pe.wait_ge(pt_d.sem, HEADS * u + n + pt_d.base)
                            pe.wait_ge(pt_a.sem, HEADS * u + n + pt_a.base)
                        pe.wait_ge(probs.sem, HEADS * u + n + 1 + probs.base)
                        for k in range(0 if windowed else 3, 4):
                            pe.transpose(bank[4][:, k * P:(k + 1) * P], sm[n % 2][:, k * P:(k + 1) * P],
                                         self.c("ident", P))
                        pe.transpose(bank[5][:, 0:P], sm[n % 2][:, 4 * P:5 * P],
                                     self.c("ident", P)).then_inc(pt.sem, 1)

                    def mix(n):
                        p, j = HP[n]
                        pe.wait_ge(pt_d.sem, HEADS * u + n + 1 + pt_d.base)
                        pe.wait_ge(pt_a.sem, HEADS * u + n + 1 + pt_a.base)
                        if n == 0 and not (first and s == 0):
                            pe.wait_ge(o_used.sem, u + o_used.base)
                        cv = slice(HD * p, HD * p + HD)
                        own = [(k, vs[s][:, k, cv]) for k in range(3)] if windowed else []
                        own += [(3 + k, v_at[:, k, cv]) for k in range(2)]
                        for m, (k, v) in enumerate(own):
                            ins = pe.matmul(obank[:, 2 * j + p, :], ptt[n % 2][:, k, :], v,
                                            start=(m == 0), stop=(m == len(own) - 1))
                        ins.then_inc(o_ready.sem, 1)
                    pe.wait_ge(staged.sem, 3 * u + 3 + staged.base)
                    score(0)
                    score(1)
                    for n in range(HEADS):
                        turn(n)
                        if n + 2 < HEADS:
                            score(n + 2)
                        mix(n)
                    pe.wait_ge(o_used.sem, u + 1 + o_used.base)
                    if not (first and s == 0):
                        pe.wait_ge(yt_used.sem, u + yt_used.base)
                    for j in range(PAIRS):
                        ins = pe.transpose(tbank[:, j, :],
                                           yn[s][:, 2 * j:2 * j + 2, :].rearrange("p h v -> p (h v)"),
                                           self.c("ident", P))
                    ins.then_inc(yt_ready.sem, 1)
                run(ENGINE.PE, body)

            @block.scalar
            def _(act):
                def body(s, i, u, b, windowed, first):
                    def out_of_psum(n):
                        p, j = HP[n]
                        h = sm[n % 2]
                        act.wait_ge(scores.sem, HEADS * u + n + 1 + scores.base)
                        if n >= 2 or not (first and s == 0):
                            act.wait_ge(pt.sem, HEADS * u + (n - 1) + pt.base)
                        act.copy(h[:, 4 * P:5 * P], bank[2 * p + 1][:, 0:P]).then_inc(center.sem, 1)
                        act.wait_ge(masked.sem, HEADS * u + n + 1 + masked.base)
                        if windowed:
                            act.copy(h[:, 0:4 * P].rearrange("p (c x) -> p c x", x=2 * P)[:, :, P:2 * P],
                                     bank[2 * p][:, :].rearrange("p (c x) -> p c x", x=2 * P)[:, :, P:2 * P]
                                     ).then_inc(center.sem, 1)
                        else:
                            act.copy(h[:, 3 * P:4 * P], bank[2 * p][:, 3 * P:4 * P]).then_inc(center.sem, 1)

                    def exps(n):
                        p, j = HP[n]
                        lo = 0 if windowed else 3 * P
                        h = sm[n % 2][:, lo:5 * P]
                        act.wait_ge(nmax.sem, HEADS * u + n + 1 + nmax.base)
                        if n == 0 and not (first and s == 0):
                            act.wait_ge(o_used.sem, u + o_used.base)
                        act.activation(h, h, ACT.Exp, scale=HD ** -0.5, bias=nm[:, 2 * j + p:2 * j + p + 1],
                                       accum_out=den[:, 2 * j + p:2 * j + p + 1]).then_inc(probs.sem, 1)
                        act.activation(es[:, 2 * j + p:2 * j + p + 1], sink[:, 2 * j + p:2 * j + p + 1], ACT.Exp,
                                       bias=nm[:, 2 * j + p:2 * j + p + 1]).then_inc(esink.sem, 1)

                    def pt_copy(n):
                        act.wait_ge(pt.sem, HEADS * u + n + 1 + pt.base)
                        act.copy(ptt[n % 2][:, 4, :], bank[5][:, 0:P]).then_inc(pt_a.sem, 1)
                    out_of_psum(0)
                    for n in range(HEADS):
                        exps(n)
                        if n + 1 < HEADS:
                            out_of_psum(n + 1)
                        pt_copy(n)
                run(ENGINE.Activation, body)

            @block.vector
            def _(dve):
                dve.wait_ge(strips_in.sem, strips_in.at(16))

                def body(s, i, u, b, windowed, first):
                    def mask(n):
                        p, j = HP[n]
                        h = sm[n % 2]
                        lo = 0 if windowed else 3 * P
                        hn = slice(2 * j + p, 2 * j + p + 1)
                        dve.wait_ge(scores.sem, HEADS * u + n + 1 + scores.base)
                        if n >= 2 or not (first and s == 0):
                            dve.wait_ge(pt.sem, HEADS * u + (n - 1) + pt.base)
                        if windowed:
                            dve.tensor_tensor(h[:, 0:4 * P].rearrange("p (c x) -> p c x", x=2 * P)[:, :, 0:P],
                                              bank[2 * p][:, :].rearrange("p (c x) -> p c x", x=2 * P)[:, :, 0:P],
                                              strips[:, :, bass.ds(b * P, P)], ALU.add).then_inc(masked.sem, 1)
                        else:
                            dve.tensor_copy(h[:, 0:1], nsink[:, 0:1]).then_inc(masked.sem, 1)
                        dve.wait_ge(masked.sem, HEADS * u + n + 1 + masked.base)
                        dve.wait_ge(center.sem, 2 * (HEADS * u + n + 1) + center.base)
                        dve.reduce_max(rmax[:, hn], h[:, lo:5 * P], AX.X).then_inc(order.sem, 1)
                        dve.wait_ge(order.sem, HEADS * u + n + 1 + order.base)
                        dve.scalar_tensor_tensor(out=nm[:, hn], in0=rmax[:, hn], scalar=-HD ** -0.5, in1=nsink[:, hn],
                                                 op0=ALU.mult, op1=ALU.min).then_inc(nmax.sem, 1)

                    def pt_copy(n):
                        lo = 0 if windowed else 3
                        dve.wait_ge(pt.sem, HEADS * u + n + 1 + pt.base)
                        if n >= 2 or not (first and s == 0):
                            dve.wait_ge(o_ready.sem, HEADS * u + (n - 1) + o_ready.base)
                        dve.tensor_copy(ptt[n % 2][:, lo:4, :], bank[4][:, lo * P:4 * P].rearrange(
                            "p (n q) -> p n q", q=P)).then_inc(pt_d.sem, 1)
                    mask(0)
                    for n in range(HEADS):
                        if n + 1 < HEADS:
                            mask(n + 1)
                        pt_copy(n)
                    dve.wait_ge(esink.sem, HEADS * u + HEADS + esink.base)
                    dve.wait_ge(probs.sem, HEADS * u + HEADS + probs.base)
                    dve.tensor_tensor(rden, den, es, ALU.add).then_inc(inv.sem, 1)
                    dve.wait_ge(inv.sem, 2 * u + 1 + inv.base)
                    dve.reciprocal(rden, rden).then_inc(inv.sem, 1)
                    dve.wait_ge(inv.sem, 2 * u + 2 + inv.base)
                    dve.wait_ge(o_ready.sem, HEADS * u + HEADS + o_ready.base)
                    dve.tensor_tensor(yn[s], obank, rden.unsqueeze(2).to_broadcast([P, HEADS, HD]),
                                      ALU.mult).then_inc(o_used.sem, 1)
                    dve.wait_ge(yt_ready.sem, u + 1 + yt_ready.base)
                    if not first:
                        dve.wait_ge(y_out[s].sem, 16 * i + y_out[s].base)
                    dve.tensor_tensor(yo[s], tbank, tiles[:, T_AGATE:T_AGATE + PAIRS, bass.ds(cols(b, windowed), P)],
                                      ALU.mult).then_inc(yt_used.sem, 1)
                run(ENGINE.DVE, body)
        strips_in.close(16), staged.close(3 * blocks), inv.close(2 * blocks)
        for x in y_out:
            x.close(8 * blocks)
        for x in (scores, masked, nmax, probs, esink, pt, pt_d, pt_a, o_ready, order):
            x.close(HEADS * blocks)
        center.close(2 * HEADS * blocks)
        for x in (o_used, yt_ready, yt_used):
            x.close(blocks)

    def project_second(self, layer):
        nc, d, tiles = self.nc, self.d, self.tiles
        keep = layer < DEPTH - 1
        free, gate, order, lora_in = (self.sig(n) for n in ("acc_free", "gates", "order_dve", "lora_in"))
        ksq, ksum, kmax, kroot, bonus_in, bonus_ready = (
            self.sig(n) for n in ("ksq", "ksum", "kmax", "kroot", "bonus_in", "bonus_ready"))
        kk = self.kk = self.ex(0, PAIRS * T).rearrange("p (j t) -> p j t", j=PAIRS)
        rk = self.ex(3840, PAIRS * T).rearrange("p (j t) -> p j t", j=PAIRS)
        norm = self.ex(7680, PAIRS * T).rearrange("p (j t) -> p j t", j=PAIRS)
        sq = self.ex(11520, PAIRS * T).rearrange("p (j t) -> p j t", j=PAIRS)
        ring = [self.ex(15360 + s * DM, DM).rearrange("p (k n) -> p k n", k=KT) for s in range(2)]
        self.bonus = self.ex(17408, NT * HEADS).rearrange("p (n h) -> p n h", h=HEADS)
        self.lora = self.ex(17472, 2 * RW).rearrange("p (s v) -> p s v", s=2)
        stream = 3 * (N2 - 1) + len(GROUPS)
        bbank = bank = self.bank[7][:, 0:NT * HEADS].rearrange("p (n h) -> p n h", h=HEADS)
        with nc.Block() as block:
            @block.sync
            def _(sp):
                sp.dma_start(self.lora, d["lora"][layer]).then_inc(lora_in.sem, 16)
                self.stream_sync(sp, d["w_2"][layer], N2, ring, 3)
                sp.wait_ge(lora_in.sem, lora_in.at(16))

            @block.tensor
            def _(pe):
                self.stream_pe(pe, self.hT, N2, ring, GROUPS, GROUPS)
                for j in range(PAIRS):
                    pe.wait_ge(ksq.sem, ksq.at(j + 1))
                    for q, (a, b) in enumerate(GROUPS):
                        m = 3 * j + q
                        if m < 3:
                            pe.wait_ge(free.sem, free.at(stream))
                        else:
                            pe.wait_ge(kroot.sem, kroot.at(m - 2))
                        pe.matmul(self.bank[m % 3][:, 0:b - a], self.c("headsum", P), sq[:, j, a:b],
                                  start=True, stop=True).then_inc(ksum.sem, 1)
                pe.wait_ge(bonus_in.sem, bonus_in.at(1))
                for n in range(NT):
                    for j in range(PAIRS):
                        ins = pe.matmul(bbank[:, n, 2 * j:2 * j + 2], rk[:, j, n * P:(n + 1) * P],
                                        self.c("headsel", 2), start=True, stop=True)
                ins.then_inc(bonus_ready.sem, 1)

            @block.scalar
            def _(act):
                self.stream_act(act, tiles, N2, GROUPS, GROUPS)
                act.wait_ge(free.sem, free.at(stream))
                act.activation(tiles[:, T_WD, :], tiles[:, T_WD, :], ACT.Tanh).then_inc(gate.sem, 1)
                act.activation(tiles[:, T_G:T_G + PAIRS, :], tiles[:, T_G:T_G + PAIRS, :], ACT.Silu).then_inc(gate.sem, 1)
                for j in range(PAIRS):
                    for q, (a, b) in enumerate(GROUPS):
                        m = 3 * j + q
                        act.wait_ge(ksum.sem, ksum.at(m + 1))
                        act.activation(norm[:, j, a:b], self.bank[m % 3][:, 0:b - a], ACT.Copy).then_inc(kroot.sem, 1)
                act.wait_ge(kmax.sem, kmax.at(1))
                act.activation(norm, norm, ACT.Sqrt).then_inc(kroot.sem, 1)

            @block.vector
            def _(dve):
                o = Order(dve, order)
                k, r = tiles[:, T_RK:T_RK + PAIRS, :], tiles[:, T_R:T_R + PAIRS, :]
                dve.wait_ge(free.sem, free.at(18))
                for j in range(PAIRS):
                    o.link(dve.tensor_scalar(kk[:, j, :], k[:, j, :], self.pr(layer, "k_k", 1, j), None, ALU.mult))
                    dve.tensor_tensor(sq[:, j, :], kk[:, j, :], kk[:, j, :], ALU.mult).then_inc(ksq.sem, 1)
                for j in range(PAIRS):
                    o(dve.tensor_scalar(rk[:, j, :], r[:, j, :], self.pr(layer, "r_k", 1, j), None, ALU.mult))
                o.wait()
                dve.tensor_tensor(rk, rk, k, ALU.mult).then_inc(bonus_in.sem, 1)
                dve.wait_ge(kroot.sem, kroot.at(9))
                dve.tensor_scalar(norm, norm, 1e-12, None, ALU.max).then_inc(kmax.sem, 1)
                dve.wait_ge(kroot.sem, kroot.at(10))
                o.link(dve.reciprocal(norm, norm))
                o.link(dve.tensor_tensor(kk, kk, norm, ALU.mult))
                dve.wait_ge(bonus_ready.sem, bonus_ready.at(1))
                o.link(dve.tensor_copy(self.bonus, bbank))
                self.total_order = o.n
        order.close(self.total_order)
        self.stream_close(N2, stream)
        lora_in.close(16), gate.close(2), ksq.close(3), ksum.close(9), kmax.close(1), kroot.close(10)
        bonus_in.close(1), bonus_ready.close(1)

    def decays(self, layer, way):
        nc, tiles = self.nc, self.tiles
        lo_in, lo_used, cum, ends, ones_col, order, done = (self.sig(n) for n in (
            "lora_ready", "lora_used", "cumulated", "exps", "ones_col", "order_dve", "scaled"))
        self.EP = self.ex(3840, PAIRS * NCH * 65).rearrange("p (j c t) -> p j c t", j=PAIRS, c=NCH)
        self.Bs = self.ex(7740, PAIRS * T).rearrange("p (j t) -> p j t", j=PAIRS)
        self.Ks = self.ex(11580, PAIRS * T).rearrange("p (j t) -> p j t", j=PAIRS)
        off, unit = (1, 0) if way == 0 else (0, CHUNK)
        th = tiles[:, 11:11 + PAIRS, :]
        ta = self.hid[:, 0:PAIRS * T].rearrange("p (j t) -> p j t", j=PAIRS)
        en = self.hid[:, 3840:3840 + 2 * T].rearrange("p (s t) -> p s t", s=2)
        rows = slice(HD * way, HD * way + HD)
        EP, Bs, Ks, kk = self.EP, self.Bs, self.Ks, self.kk
        with nc.Block() as block:
            @block.tensor
            def _(pe):
                for j in range(PAIRS):
                    for s, src in ((0, T_WD), (1, T_AD)):
                        for q, (a, b) in enumerate(GROUPS):
                            if j > 0:
                                pe.wait_ge(lo_used.sem, lo_used.at(6 * (j - 1) + 3 * s + q + 1))
                            pe.matmul(self.bank[3 * s + q][:, 0:b - a], self.lora[rows, s, j * P:(j + 1) * P],
                                      tiles[rows, src, a:b], start=True, stop=True).then_inc(lo_in.sem, 1)

            @block.scalar
            def _(act):
                for j in range(PAIRS):
                    for s, dst, bias in ((0, th, "hw0"), (1, ta, "ha0")):
                        for q, (a, b) in enumerate(GROUPS):
                            act.wait_ge(lo_in.sem, lo_in.at(6 * j + 3 * s + q + 1))
                            act.activation(dst[:, j, a:b], self.bank[3 * s + q][:, 0:b - a], ACT.Tanh, scale=0.5,
                                           bias=self.dv(layer, bias, 1, PAIRS * way + j)).then_inc(lo_used.sem, 1)
                for j in range(PAIRS):
                    cs = th[:, j, :].rearrange("p (c t) -> p c t", t=CHUNK)
                    act.wait_ge(cum.sem, cum.at(5 * j + 5))
                    act.activation(EP[:, j, :, off:off + CHUNK], cs, ACT.Exp, scale=-DECAY).then_inc(ends.sem, 1)
                    if j >= 2:
                        act.wait_ge(done.sem, done.at(2 * (j - 1)))
                    act.activation(en[:, j % 2, :], th[:, j, :], ACT.Exp, scale=DECAY).then_inc(ends.sem, 1)

            @block.gpsimd
            def _(pool):
                pool.memset(EP[:, :, :, unit:unit + 1], 1.0).then_inc(ones_col.sem, 1)
                pool.wait_ge(ones_col.sem, ones_col.at(1))

            @block.vector
            def _(dve):
                o = Order(dve, order)
                for j in range(PAIRS):
                    dve.wait_ge(lo_used.sem, lo_used.at(6 * j + 3))
                    o.link(dve.tensor_scalar(th[:, j, :], th[:, j, :], 1.0, None, ALU.add))
                    run = th[:, j, :] if way == 0 else th[:, j, ::-1]
                    for q in range(T // 256):
                        part = run[:, q * 256:(q + 1) * 256]
                        dve.tensor_tensor_scan(out=part, data0=self.c("reset", 256), data1=part, initial=0.0,
                                               op0=ALU.mult, op1=ALU.add).then_inc(cum.sem, 1)
                for j in range(PAIRS):
                    dve.wait_ge(lo_used.sem, lo_used.at(6 * j + 6))
                    o(dve.scalar_tensor_tensor(out=Bs[:, j, :], in0=ta[:, j, :], scalar=1.0, in1=kk[:, j, :],
                                               op0=ALU.add, op1=ALU.mult))
                    o.wait()
                    o.link(dve.tensor_scalar(ta[:, j, :], ta[:, j, :], -1.0, self.dv(layer, "hk_a", 1, j),
                                             ALU.add, ALU.mult))
                    o.link(dve.scalar_tensor_tensor(out=Ks[:, j, :], in0=ta[:, j, :], scalar=1.0,
                                                    in1=tiles[:, T_RK + j, :], op0=ALU.add, op1=ALU.mult))
                    dve.wait_ge(ends.sem, ends.at(2 * j + 2))
                    dve.scalar_tensor_tensor(out=Bs[:, j, :], in0=Bs[:, j, :], scalar=0.5, in1=en[:, j % 2, :],
                                             op0=ALU.mult, op1=ALU.mult).then_inc(done.sem, 1)
                    dve.tensor_tensor(Ks[:, j, :], Ks[:, j, :], en[:, j % 2, :], ALU.mult).then_inc(done.sem, 1)
                self.total_order = o.n
        order.close(self.total_order)
        lo_in.close(18), lo_used.close(18), cum.close(15), ends.close(6), ones_col.close(1), done.close(6)

    def scan(self, layer, way):
        nc, d, tiles, bank = self.nc, self.d, self.tiles, self.bank
        prep, trs, tr_out, amat, amat_out, joins, xt0, w_rdy, w_out, xx_rdy, xx_out, u0, u0_out, wu, wu_out, \
            gr, g_out, h_out, r_out, yi, yi_out, yi_sum, st, st_out, yo, yo_out, x0 = (self.sig(n) for n in (
                "prep", "turned", "turned_out", "amat", "amat_out", "joins", "xt_start", "w_ready", "w_out",
                "xx_ready", "xx_out", "u0", "u0_out", "wu", "wu_out", "ghr", "g_out", "h_out", "r_out", "yi",
                "yi_out", "yi_sum", "state", "state_out", "yo", "yo_out", "x_start"))
        v_in = [self.sig(f"v_in{s}") for s in range(2)]
        spaces = [[self.hid, 0, 6400], [self.tiles[:, 11:16, :].rearrange("p n t -> p (n t)"), 0, 6400],
                  [self.extra, 15480, 17400]]

        def take(n):
            for s in spaces:
                if s[1] + n <= s[2]:
                    s[1] += n
                    return s[0][:, s[1] - n:s[1]]
            raise ValueError("no room")
        jct = dict(j=PAIRS, c=2)
        ntl = take(5 * RW).rearrange("p (l n) -> p l n", l=5)
        kkr = [take(2 * RW).rearrange("p (j s c t) -> p j s c t", s=2, **jct) for _ in range(2)]
        bch, kch, bend, kend, vs = ([take(RW) for _ in range(2)] for _ in range(5))
        pend = [take(2 * PAIRS).rearrange("p (j c) -> p j c", j=PAIRS) for _ in range(2)]
        rhs = take(2 * RW).rearrange("p (h s v) -> p h s v", h=HEADS, s=2)
        nbt, kt_ = take(RW), take(RW)
        nbm, kbm = (take(2 * RW).rearrange("p (q j s t) -> p q j s t", q=2, j=PAIRS, s=2) for _ in range(2))
        xx = take(2 * RW).rearrange("p (q s j t) -> p q s j t", q=2, s=2, j=PAIRS)
        wb = take(RW).rearrange("p (q j t) -> p q j t", q=2, j=PAIRS)
        wus = take(2 * RW).rearrange("p (h s v) -> p h s v", h=HEADS, s=2)
        gs, hs, rt = ([take(RW // 2).rearrange("p (j t) -> p j t", j=PAIRS) for _ in range(2)] for _ in range(3))
        yis = take(RW).rearrange("p (h v) -> p h v", h=HEADS)
        state = take(RW // 2).rearrange("p (j v) -> p j v", j=PAIRS)
        yacc = self.yacc = self.hid[:, 6400:6400 + NT * RW].rearrange("p (n h v) -> p n h v", n=NT, h=HEADS)
        EP, Bs, Ks, kk = self.EP, self.Bs, self.Ks, self.kk
        excl, incl, last = (0, 1, CHUNK) if way == 0 else (1, 0, 0)
        order_c = (0, 1) if way == 0 else (1, 0)
        half = [slice(HD * x, HD * x + HD) for x in range(2)]
        heads = [(j, p) for p in range(2) for j in range(PAIRS)]
        id64 = self.c("id64", HD)
        NL = len(LEVELS)

        def over_pairs(x):
            return x.unsqueeze(1).to_broadcast([P, PAIRS, x.shape[1]])

        def run(engine, body):
            for s in range(2):
                body(s, 0, s, s if way == 0 else 1 - s, True)
            with self.loop(engine, 1, NT // 2) as i:
                taus = [2 * i + s if way == 0 else i * -2 + (NT + 1 - s) for s in range(2)]
                for s in range(2):
                    body(s, i, 2 * i + s, taus[s], False)

        def bank3(i):
            return bank[i][:, 0:RW // 2].rearrange("p (j t) -> p j t", j=PAIRS)

        with nc.Block() as block:
            @block.sync
            def _(sp):
                def body(s, i, u, tau, first):
                    if not first:
                        sp.wait_ge(yo_out.sem, 2 * (u - 1) + yo_out.base)
                    sp.dma_start(vs[s], d["v_rw"][bass.ds(tau, 1)].rearrange("a p v -> (a p) v")).then_inc(v_in[s].sem, 16)
                run(ENGINE.SP, body)

            @block.gpsimd
            def _(pool):
                def body(s, i, u, tau, first):
                    def chunks(x):
                        return x.rearrange("p j (c t) -> p j c t", t=CHUNK)[:, :, bass.ds(2 * tau, 2), :]

                    def own(x):
                        return x.rearrange("p (j c t) -> p j c t", t=CHUNK, **jct)
                    if not first:
                        pool.wait_ge(yo_out.sem, 2 * (u - 1) + yo_out.base)
                    ep = EP[:, :, bass.ds(2 * tau, 2), :]
                    pend_b = ep[:, :, :, last:last + 1].to_broadcast([P, PAIRS, 2, CHUNK])
                    for ins in (
                        pool.tensor_tensor(kkr[s][:, :, 0], chunks(kk), ep[:, :, :, excl:excl + CHUNK], ALU.mult),
                        pool.tensor_tensor(own(bend[s]), chunks(Bs), pend_b, ALU.mult),
                        pool.tensor_tensor(own(kend[s]), chunks(Ks), pend_b, ALU.mult),
                        pool.tensor_tensor(kkr[s][:, :, 1], chunks(tiles[:, T_R:T_R + PAIRS, :]),
                                           ep[:, :, :, incl:incl + CHUNK], ALU.mult),
                        pool.tensor_copy(own(bch[s]), chunks(Bs)),
                        pool.tensor_copy(own(kch[s]), chunks(Ks)),
                        pool.tensor_copy(pend[s].unsqueeze(3), ep[:, :, :, last:last + 1]),
                    ):
                        ins.then_inc(prep.sem, 1)
                    for q in range(2):
                        pool.wait_ge(amat_out.sem, 4 * u + q + 1 + amat_out.base)
                        pool.tensor_tensor(xx[:, q, 1], nbm[:, q, :, 0, :], over_pairs(self.c("join1", HD)),
                                           ALU.mult).then_inc(xt0.sem, 1)
                    for q in range(2):
                        pool.wait_ge(xt0.sem, 4 * u + q + 1 + xt0.base)
                        pool.tensor_tensor(xx[:, q, 1], xx[:, q, 1], over_pairs(id64), ALU.add).then_inc(xt0.sem, 1)
                    for l in range(NL):
                        for q in range(2):
                            m = self.c("join", 5 * HD)[:, l * HD:(l + 1) * HD]
                            pool.tensor_tensor(ntl[:, l, q * 192:(q + 1) * 192].rearrange("p (j t) -> p j t", j=PAIRS),
                                               nbm[:, q, :, 0, :], over_pairs(m), ALU.mult).then_inc(joins.sem, 1)
                    if way:
                        pool.wait_ge(yi_out.sem, u + 1 + yi_out.base)
                        pool.tensor_tensor(yis, yis, yacc[:, bass.ds(tau, 1)].rearrange("p a h v -> p (a h) v"),
                                           ALU.add).then_inc(yi_sum.sem, 1)
                run(ENGINE.Pool, body)

            @block.tensor
            def _(pe):
                def body(s, i, u, tau, first):
                    again = not (first and s == 0)

                    def hold(x, per_unit, more):
                        count = per_unit * u + more + x.base
                        if not first:
                            count = pe.to_reg(count)
                            pe.wait_ge(x.sem, x.at(2 * per_unit + more))
                        pe.wait_ge(x.sem, count)
                    hold(prep, 7, 3)
                    if again:
                        hold(yo_out, 2, 0)
                        hold(st_out, 2, 1)
                    for m, src in enumerate((None, bend[s], kend[s])):
                        for j in range(PAIRS):
                            x = kkr[s][:, j, 0].rearrange("p c t -> p (c t)") if m == 0 else src[:, j * P:(j + 1) * P]
                            ins = pe.transpose(bank[m][:, j * P:(j + 1) * P], x, self.c("ident", P))
                        ins.then_inc(trs.sem, 1)
                    hold(prep, 7, 6)
                    for b0, left in ((3, bch[s]), (5, kch[s])):
                        for p in range(2):
                            for j in range(PAIRS):
                                for c in range(2):
                                    ins = pe.matmul(bank[b0 + p][half[c], j * P:(j + 1) * P],
                                                    left[half[p], (2 * j + c) * HD:(2 * j + c + 1) * HD],
                                                    kkr[s][half[p], j, :, c, :], start=True, stop=True)
                            ins.then_inc(amat.sem, 1)
                    for p in range(2):
                        if p:
                            hold(tr_out, 3, 1)
                        for j in range(PAIRS):
                            for c in range(2):
                                ins = pe.matmul(bank[7 - 7 * p][half[c], j * HD:(j + 1) * HD], kkr[s][half[p], j, 0, c, :],
                                                bch[s][half[p], (2 * j + c) * HD:(2 * j + c + 1) * HD],
                                                start=True, stop=True)
                        ins.then_inc(amat.sem, 1)
                    hold(v_in[s], 8, 16 - 8 * s)
                    hold(amat_out, 4, 4)
                    for j, p in heads:
                        h = 2 * j + p
                        for c in range(2):
                            ins = pe.matmul(bank[5][half[c], h * HD:(h + 1) * HD], kbm[half[c], p, j, 0, :],
                                            vs[s][half[c], h * HD:(h + 1) * HD], start=True, stop=True)
                    ins.then_inc(u0.sem, 1)
                    hold(tr_out, 3, 3)
                    for l in range(NL):
                        for p in range(2):
                            if l == 0:
                                hold(x0, 4, 3 + p)
                                hold(xt0, 4, 3 + p)
                            else:
                                hold(xx_out, 2 * NL, 2 * (l - 1) + p + 1)
                            hold(joins, 2 * NL, 2 * l + p + 1)
                            for j in range(PAIRS):
                                for c in range(2):
                                    a = p * 192 + j * HD
                                    ins = pe.matmul(bank[1 + p][half[c], j * HD:(j + 1) * HD], ntl[half[c], l, a:a + HD],
                                                    xx[half[c], p, 0, j, :], start=True, stop=True)
                            ins.then_inc(w_rdy.sem, 1)
                        for p in range(2):
                            hold(w_out, 2 * NL, 2 * l + p + 1)
                            for j in range(PAIRS):
                                for c in range(2):
                                    if l < NL - 1:
                                        pe.matmul(bank[3 + p][half[c], j * HD:(j + 1) * HD], xx[half[c], p, 1, j, :],
                                                  wb[half[c], p, j, :], start=True, stop=True)
                                    ins = pe.matmul(bank[3 + p][half[c], (3 + j) * HD:(4 + j) * HD],
                                                    wb[half[c], p, j, :], xx[half[c], p, 1, j, :], start=True, stop=True)
                            ins.then_inc(xx_rdy.sem, 1)
                    hold(u0_out, 1, 1)
                    for p in range(2):
                        hold(xx_out, 2 * NL, 2 * (NL - 1) + p + 1)
                        for j in range(PAIRS):
                            for c in range(2):
                                ins = pe.matmul(bank[6 + p][half[c], j * P:(j + 1) * P], xx[half[c], p, 1, j, :],
                                                rhs[half[c], 2 * j + p], start=True, stop=True)
                        ins.then_inc(wu.sem, 1)
                    hold(wu_out, 2, 2)
                    for c in order_c:
                        for j, p in heads:
                            h = 2 * j + p
                            ins = pe.matmul(bank[c][half[p], j * HD:(j + 1) * HD], wus[half[c], h, 0, :],
                                            nbt[half[c], h * HD:(h + 1) * HD], start=True, stop=True)
                        ins.then_inc(gr.sem, 1)
                        for j, p in heads:
                            h = 2 * j + p
                            hc = slice(h * HD, (h + 1) * HD)
                            pe.matmul(bank[2 + c][half[p], j * HD:(j + 1) * HD], kt_[half[c], hc], vs[s][half[c], hc],
                                      start=True, stop=False)
                            ins = pe.matmul(bank[2 + c][half[p], j * HD:(j + 1) * HD], nbt[half[c], hc],
                                            wus[half[c], h, 1, :], start=False, stop=True)
                        ins.then_inc(gr.sem, 1)
                        for j, p in heads:
                            ins = pe.matmul(bank[4 + c][half[p], j * HD:(j + 1) * HD], wus[half[c], 2 * j + p, 0, :],
                                            nbm[half[c], p, j, 1, :], start=True, stop=True)
                        ins.then_inc(gr.sem, 1)
                    for j, p in heads:
                        h = 2 * j + p
                        for c in range(2):
                            pe.matmul(bank[6][half[c], h * HD:(h + 1) * HD], kbm[half[c], p, j, 1, :],
                                      vs[s][half[c], h * HD:(h + 1) * HD], start=True, stop=False)
                            ins = pe.matmul(bank[6][half[c], h * HD:(h + 1) * HD], nbm[half[c], p, j, 1, :],
                                            wus[half[c], h, 1, :], start=False, stop=True)
                    ins.then_inc(yi.sem, 1)
                    hold(g_out, 6, 6)
                    hold(h_out, 2, 2)
                    hold(r_out, 2, 2)
                    for m, c in enumerate(order_c):
                        hold(st_out, 2, m + 1)
                        for j, p in heads:
                            ins = pe.matmul(bank[1 + m][half[p], j * HD:(j + 1) * HD], gs[c][half[p], j, :],
                                            state[half[p], j, :], start=True, stop=True)
                        for j, p in heads:
                            ins = pe.matmul(bank[7 - 7 * p][half[c], j * HD:(j + 1) * HD], rt[c][half[p], j, :],
                                            state[half[p], j, :], start=True, stop=True)
                        ins.then_inc(st.sem, 1)
                run(ENGINE.PE, body)

            @block.scalar
            def _(act):
                def body(s, i, u, tau, first):
                    for m, (dst, scale) in enumerate(((rhs[:, :, 0, :], 1.0), (nbt, -1.0), (kt_, 1.0))):
                        act.wait_ge(trs.sem, 3 * u + m + 1 + trs.base)
                        src = bank[m][:, 0:RW]
                        if m == 0:
                            src = src.rearrange("p (h v) -> p h v", h=HEADS)
                        act.activation(dst, src, ACT.Copy, scale=scale).then_inc(tr_out.sem, 1)
                    for l in range(NL):
                        for p in range(2):
                            act.wait_ge(xx_rdy.sem, 2 * NL * u + 2 * l + p + 1 + xx_rdy.base)
                            a = 0 if l < NL - 1 else 1
                            act.copy(xx[:, p, a:2], bank[3 + p][:, 192 * a:384].rearrange(
                                "p (s j t) -> p s j t", j=PAIRS, t=HD)).then_inc(xx_out.sem, 1)
                    for p in range(2):
                        act.wait_ge(wu.sem, 2 * u + p + 1 + wu.base)
                        act.copy(wus.rearrange("p (j q) s v -> p j q (s v)", q=2)[:, :, p, :],
                                 bank[6 + p][:, 0:RW].rearrange("p (j x) -> p j x", j=PAIRS)).then_inc(wu_out.sem, 1)
                    for m, c in enumerate(order_c):
                        act.wait_ge(gr.sem, 6 * u + 3 * m + 2 + gr.base)
                        act.copy(hs[c], bank3(2 + c)).then_inc(h_out.sem, 1)
                    act.wait_ge(yi.sem, u + 1 + yi.base)
                    if not (first and s == 0):
                        act.wait_ge(yo_out.sem, 2 * u + yo_out.base)
                    act.copy(yis, bank[6][:, 0:RW].rearrange("p (h v) -> p h v", h=HEADS)).then_inc(yi_out.sem, 1)
                run(ENGINE.Activation, body)

            @block.vector
            def _(dve):
                dve.memset(state, 0.0).then_inc(st_out.sem, 1)

                def body(s, i, u, tau, first):
                    for b0, dst, mask in ((3, nbm, f"maskB{way}"), (5, kbm, f"maskK{way}")):
                        for p in range(2):
                            dve.wait_ge(amat.sem, 6 * u + (b0 - 3) + p + 1 + amat.base)
                            dve.tensor_tensor(dst[:, p].rearrange("p j s t -> p j (s t)"),
                                              bank[b0 + p][:, 0:RW].rearrange("p (j x) -> p j x", j=PAIRS),
                                              over_pairs(self.c(mask, 2 * HD)), ALU.mult).then_inc(amat_out.sem, 1)
                    for p in range(2):
                        dve.wait_ge(amat.sem, 6 * u + 5 + p + amat.base)
                        dve.tensor_tensor(xx[:, p, 0], bank3(7 - 7 * p), over_pairs(self.c(f"maskN{way}", HD)),
                                          ALU.mult).then_inc(x0.sem, 1)
                    for p in range(2):
                        dve.wait_ge(x0.sem, 4 * u + p + 1 + x0.base)
                        dve.tensor_tensor(xx[:, p, 0], xx[:, p, 0], over_pairs(id64), ALU.add).then_inc(x0.sem, 1)
                    dve.wait_ge(u0.sem, u + 1 + u0.base)
                    dve.tensor_copy(rhs[:, :, 1, :], bank[5][:, 0:RW].rearrange("p (h v) -> p h v", h=HEADS)
                                    ).then_inc(u0_out.sem, 1)
                    for l in range(NL):
                        for p in range(2):
                            dve.wait_ge(w_rdy.sem, 2 * NL * u + 2 * l + p + 1 + w_rdy.base)
                            dve.tensor_tensor(wb[:, p], bank3(1 + p), over_pairs(id64), ALU.add).then_inc(w_out.sem, 1)
                    dve.wait_ge(prep.sem, 7 * u + 7 + prep.base)
                    for m, c in enumerate(order_c):
                        dve.wait_ge(gr.sem, 6 * u + 3 * m + 1 + gr.base)
                        for j in range(PAIRS):
                            dve.scalar_tensor_tensor(out=gs[c][:, j, :], in0=id64, scalar=pend[s][:, j, c:c + 1],
                                                     in1=bank3(c)[:, j, :], op0=ALU.mult, op1=ALU.add
                                                     ).then_inc(g_out.sem, 1)
                        dve.wait_ge(gr.sem, 6 * u + 3 * m + 3 + gr.base)
                        dve.tensor_tensor(rt[c], bank3(4 + c), kkr[s][:, :, 1, c, :], ALU.add).then_inc(r_out.sem, 1)
                    for m, c in enumerate(order_c):
                        dve.wait_ge(st.sem, 2 * u + m + 1 + st.base)
                        dve.wait_ge(h_out.sem, 2 * u + m + 1 + h_out.base)
                        dve.tensor_tensor(state, bank3(1 + m), hs[c], ALU.add).then_inc(st_out.sem, 1)
                    if way:
                        dve.wait_ge(yi_sum.sem, u + 1 + yi_sum.base)
                    else:
                        dve.wait_ge(yi_out.sem, u + 1 + yi_out.base)
                    part = yacc[:, bass.ds(tau, 1)].rearrange("p a (j q) v -> p (a j) q v", q=2)
                    for p in range(2):
                        dve.tensor_tensor(part[:, :, p, :], bank3(7 - 7 * p),
                                          yis.rearrange("p (j q) v -> p j q v", q=2)[:, :, p, :],
                                          ALU.add).then_inc(yo_out.sem, 1)
                run(ENGINE.DVE, body)
        n = NT
        for x, k in ((v_in[0], 8), (v_in[1], 8), (prep, 7), (trs, 3), (tr_out, 3), (amat, 6), (amat_out, 4), (joins, 2 * NL), (xt0, 4),
                     (x0, 4), (w_rdy, 2 * NL), (w_out, 2 * NL), (xx_rdy, 2 * NL), (xx_out, 2 * NL), (u0, 1), (u0_out, 1),
                     (wu, 2), (wu_out, 2), (gr, 6), (g_out, 6), (h_out, 2), (r_out, 2), (yi, 1), (yi_out, 1),
                     (yi_sum, way), (st, 2), (yo_out, 2)):
            x.close(k * n)
        st_out.close(2 * n + 1)

    def readout(self, layer):
        nc, d, tiles = self.nc, self.d, self.tiles
        keep = layer < DEPTH - 1
        n0 = 0 if keep else CTX // P
        cnt = NT - n0
        back, order, act_order, var_ready, y_ready, turned, done = (self.sig(n) for n in (
            "read_in", "order_dve", "var_root", "var_ready", "y_ready", "y_turned", "y_gated"))
        y = self.yacc[:, n0:, :, :].rearrange("p n h v -> p (n h) v")
        G = cnt * HEADS
        tmp = self.hid[:, 0:G * HD].rearrange("p (g v) -> p g v", v=HD)
        v = self.ex(0, G * HD).rearrange("p (g v) -> p g v", v=HD)
        ln = self.ex(3840, 2 * RW).rearrange("p (s v) -> p s v", s=2)
        mean = self.ex(3840 + 768, G)
        var = self.ex(3840 + 768 + 64, G)
        bonus = self.bonus[:, n0:, :].rearrange("p n h -> p (n h)")

        def bc(x):
            return x.unsqueeze(2).to_broadcast([P, G, HD])

        def row(s):
            return ln[:, s:s + 1, :].to_broadcast([P, cnt, RW])
        flat = y.rearrange("p (n h) v -> p n (h v)", h=HEADS)
        with nc.Block() as block:
            @block.sync
            def _(sp):
                lo = n0 * P
                sp.dma_start(ln, d["ln"][layer]).then_inc(back.sem, 16)
                sp.dma_start(v.rearrange("p (n h) v -> p n (h v)", h=HEADS),
                             d["v_rw"][n0:].rearrange("n p v -> p n v")).then_inc(back.sem, 16)
                sp.dma_start(tiles[:, 11:16, lo:T], d["y"].rearrange("n p t -> p n t")[:, :, lo:T]).then_inc(back.sem, 16)
                xsrc = d["x"] if layer == 0 else d["x_mid"]
                sp.dma_start(tiles[:, 0:KT, lo:T], xsrc[:, :, lo:T]).then_inc(back.sem, 16)
                sp.wait_ge(back.sem, back.at(64))

            @block.vector
            def _(dve):
                o = Order(dve, order)
                o.link(dve.reduce_sum(mean, y, AX.X))
                o.link(dve.tensor_scalar(mean, mean, 1.0 / HD, None, ALU.mult))
                o.link(dve.tensor_tensor(y, y, bc(mean), ALU.subtract))
                o.link(dve.tensor_tensor(tmp, y, y, ALU.mult))
                dve.reduce_sum(var, tmp, AX.X).then_inc(var_ready.sem, 1)
                dve.wait_ge(act_order.sem, act_order.at(1))
                o.link(dve.reciprocal(var, var))
                o.link(dve.tensor_tensor(y, y, bc(var), ALU.mult))
                dve.wait_ge(back.sem, back.at(64))
                o.link(dve.tensor_tensor(flat, flat, row(0), ALU.mult))
                o.link(dve.tensor_tensor(flat, flat, row(1), ALU.add))
                o.link(dve.tensor_tensor(tmp, v, bc(bonus), ALU.mult))
                dve.tensor_tensor(y, y, tmp, ALU.add).then_inc(y_ready.sem, 1)
                for n in range(n0, NT):
                    dve.wait_ge(turned.sem, turned.at(n - n0 + 1))
                    gate = tiles[:, T_G:T_G + PAIRS, n * P:(n + 1) * P]
                    dve.tensor_tensor(gate, self.bank[n % 2][:, 0:RW].rearrange("p (j t) -> p j t", j=PAIRS), gate,
                                      ALU.mult).then_inc(done.sem, 1)
                self.total_order = o.n

            @block.scalar
            def _(act):
                act.wait_ge(var_ready.sem, var_ready.at(1))
                act.activation(var, var, ACT.Sqrt, scale=1.0 / HD, bias=self.eps[:, 1:2]).then_inc(act_order.sem, 1)

            @block.tensor
            def _(pe):
                pe.wait_ge(y_ready.sem, y_ready.at(1))
                for n in range(n0, NT):
                    if n - n0 >= 2:
                        pe.wait_ge(done.sem, done.at(n - n0 - 1))
                    for j in range(PAIRS):
                        ins = pe.transpose(self.bank[n % 2][:, j * P:(j + 1) * P], flat[:, n - n0, j * P:(j + 1) * P],
                                           self.c("ident", P))
                    ins.then_inc(turned.sem, 1)
        order.close(self.total_order)
        back.close(64), act_order.close(1), var_ready.close(1), y_ready.close(1), turned.close(cnt), done.close(cnt)

    def project_out(self, layer):
        nc, d, tiles = self.nc, self.d, self.tiles
        keep = layer < DEPTH - 1
        groups = GROUPS if keep else GROUPS[1:]
        ng = len(groups)
        ready, free, x_out = (self.sig(n) for n in ("acc_ready", "acc_free", "dma_out"))
        taken = self.sig("res_free")
        ring = [self.ex(s * DM, DM).rearrange("p (k n) -> p k n", k=KT) for s in range(2)]
        with nc.Block() as block:
            @block.sync
            def _(sp):
                self.stream_sync(sp, d["w_out"][layer], KT, ring, ng)
                if keep:
                    sp.wait_ge(taken.sem, taken.at(ng * KT))
                    sp.dma_start(d["x_mid"], tiles[:, 0:KT, :]).then_inc(x_out.sem, 16)
                    sp.wait_ge(x_out.sem, x_out.at(16))

            @block.tensor
            def _(pe):
                save, self.signals["acc_free"] = self.signals["acc_free"], taken
                self.stream_pe(pe, tiles[:, KT:2 * KT, :], KT, ring, groups, groups)
                self.signals["acc_free"] = save

            @block.vector
            def _(dve):
                with self.loop(ENGINE.DVE, 0, KT // 2) as i:
                    for s in range(2):
                        t = 2 * i + s
                        for q, (a, b) in enumerate(groups):
                            gate = self.ada[:, layer, bass.ds(2 * KT + t, 1), (1 if a == 0 else 0)]
                            x = tiles[:, bass.ds(t, 1), a:b].rearrange("p n t -> p (n t)")
                            dve.wait_ge(ready.sem, ng * t + q + 1 + ready.base)
                            dve.scalar_tensor_tensor(out=x, in0=self.bank[3 * s + q][:, 0:b - a], scalar=gate,
                                                     in1=x, op0=ALU.mult, op1=ALU.add).then_inc(taken.sem, 1)
        self.sig("w_in0").close(8 * KT), self.sig("w_in1").close(8 * KT), ready.close(ng * KT), taken.close(ng * KT)
        x_out.close(16 if keep else 0)

    def final_norm(self):
        nc, d = self.nc, self.d
        sq = self.ex(0, 2 * T).rearrange("p (s t) -> p s t", s=2)
        rstd = self.ex(2 * T, T)
        x = self.tiles[:, 0:KT, :]
        roots, order, outs, stored = (self.sig(n) for n in ("roots", "order_dve", "outs", "dma_out"))
        groups = GROUPS[1:]
        with nc.Block() as block:
            self.inv_rms(block, x, sq, rstd, CTX, groups)

            @block.vector
            def _(dve):
                o = Order(dve, order)
                for n, (a, b) in enumerate(groups):
                    dve.wait_ge(roots.sem, roots.at(n + 1))
                    o(dve.reciprocal(rstd[:, a:b], rstd[:, a:b]))
                o.wait()
                for k in range(KT):
                    dve.scalar_tensor_tensor(out=x[:, k, CTX:T], in0=x[:, k, CTX:T], scalar=self.fing[:, k:k + 1],
                                             in1=rstd[:, CTX:T], op0=ALU.mult, op1=ALU.mult).then_inc(outs.sem, 1)

            @block.sync
            def _(sp):
                for k in range(KT):
                    sp.wait_ge(outs.sem, outs.at(k + 1))
                    sp.dma_start(d["out"][:, k, :], x[:, k, CTX:T]).then_inc(stored.sem, 16)
                sp.wait_ge(stored.sem, stored.at(16 * KT))


def column_order():
    sizes = (384, 384, 384, 384, 128, 128, 384, 128, 128, 384, 256, 256, 256, 256)
    starts = np.concatenate([[0], np.cumsum(sizes)[:-1]])
    r, k, v, g, wd, ad, q, ka, va, ga, bg, cg, xin, cgate = (
        np.arange(s, s + n) for s, n in zip(starts, sizes))
    first = np.concatenate([cg, xin, bg, cgate, q[head_order()], ga[head_order()], ka])
    second = np.concatenate([r, k, wd, ad, g])
    return first, second, np.concatenate([v, va])


def head_order():
    return np.concatenate([np.arange(HD) + HD * h for j in range(PAIRS) for h in (j, PAIRS + j)])


def const_table():
    out = np.zeros((P, NCONST), np.float32)

    def put(name, x):
        out[:, CONST[name]:CONST[name] + x.shape[1]] = x
    i = np.arange(P)
    put("ident", np.eye(P))
    rot = np.zeros((P, P))
    for h in (0, HD):
        for m in range(HD // 2):
            rot[h + m + HD // 2, h + m] = -1
            rot[h + m, h + m + HD // 2] = 1
    put("rot", rot)
    put("headsum", (i[:, None] // HD == i[None, :] // HD))
    put("ones", np.ones((P, P)))
    put("headsel", i[:, None] // HD == np.arange(2)[None, :])
    put("reset", np.broadcast_to(np.arange(256) % CHUNK != 0, (P, 256)))
    a, b = i[:, None] % HD, np.arange(HD)[None, :]
    put("id64", a == b)
    join = [(a // (2 * m) == b // (2 * m)) & (a // m != b // m) for m in (1,) + LEVELS]
    put("join1", join[0])
    put("join", np.concatenate(join[1:], 1))
    for way, (after, before) in enumerate(((b > a, b < a), (b < a, b > a))):
        put(f"maskB{way}", -np.concatenate([after, after | (a == b)], 1).astype(np.float32))
        put(f"maskK{way}", np.concatenate([after, after | (a == b)], 1))
        put(f"maskN{way}", -(before & join[0]).astype(np.float32))
    return out


def trig_table():
    inv = np.float32(10000.0) ** (-np.arange(HD // 4, dtype=np.float32) / np.float32(HD // 4))
    t = np.arange(SEQ)
    ang = np.concatenate([(t // 64).astype(np.float32)[:, None] * inv, (t % 64).astype(np.float32)[:, None] * inv], 1)
    freq = np.arange(P) % (HD // 2)
    return np.stack([np.cos(ang).T[freq], np.sin(ang).T[freq]], 1).astype(np.float32)


def strip_table():
    out = np.zeros((P, 2, QB, P), np.float32)
    q, k = np.arange(P)[:, None], np.arange(P)[None, :]
    out[:, 0] = np.where(k >= q, 0.0, MASK_VALUE)[:, None]
    out[:, 1] = np.where(k <= q, 0.0, MASK_VALUE)[:, None]
    out[:, 0, 0] = MASK_VALUE
    out[:, 1, QB - 1] = MASK_VALUE
    return out.reshape(P, 2, QB * P)


def kernel(x, c, ctx, c_ctx, w_ada, b_ada, norm_g, w_in, w_out, rw_w0, rw_w_up, rw_a0, rw_a_up, rw_k_k, rw_k_a,
           rw_r_k, rw_ln_g, rw_ln_b, at_sink, cv_w, final_g):
    import concourse.bacc as bacc
    from concourse.bass_utils import run_bass_kernel_spmd

    def channels(a):
        a = np.asarray(a)
        return np.moveaxis(a.reshape(a.shape[:-1] + (-1, P)), -1, 0)

    def weight_tiles(w, n):
        w = np.asarray(w)
        return w.reshape(DEPTH, KT, P, -1, n).transpose(0, 3, 2, 1, 4)
    first, second, values = column_order()
    w_in, w_out = np.asarray(w_in), np.asarray(w_out)
    rows = np.concatenate([np.arange(RW), RW + head_order(), np.arange(2 * RW, DM)])
    tokens = np.concatenate([np.asarray(ctx)[0], np.asarray(x)[0]], 0)
    param = np.concatenate([
        channels(norm_g), channels(rw_w0).reshape(P, DEPTH, -1), channels(rw_a0).reshape(P, DEPTH, -1),
        channels(rw_k_k), channels(rw_k_a), channels(np.asarray(rw_r_k).reshape(DEPTH, RW)),
        channels(cv_w).reshape(P, DEPTH, -1),
        np.broadcast_to(np.asarray(at_sink).reshape(DEPTH, 2, PAIRS).transpose(0, 2, 1).reshape(1, DEPTH, HEADS),
                        (P, DEPTH, HEADS)),
        channels(b_ada)], -1)
    lora = np.stack([np.asarray(rw_w_up).reshape(DEPTH, P, RW), np.asarray(rw_a_up).reshape(DEPTH, P, RW)], 2)
    ln = np.broadcast_to(np.stack([np.asarray(rw_ln_g), np.asarray(rw_ln_b)], 1)[:, None], (DEPTH, P, 2, RW))
    cc = np.stack([np.asarray(c)[0].reshape(KT, P).T, np.asarray(c_ctx).reshape(KT, P).T], 2)
    arrays = {
        "x": np.moveaxis(tokens.T.reshape(KT, P, T), 0, 1), "cc": cc, "const": const_table(), "param": param,
        "fing": channels(final_g), "w_ada": weight_tiles(w_ada, 512).reshape(-1, P, KT, 512),
        "w_1": weight_tiles(w_in[:, :, first], P), "w_2": weight_tiles(w_in[:, :, second], P),
        "w_v": weight_tiles(w_in[:, :, values], 512)[:, 0], "w_out": weight_tiles(w_out[:, rows], P),
        "lora": lora, "ln": ln, "trig": trig_table(), "strips": strip_table(),
    }
    arrays = {k: np.ascontiguousarray(v) for k, v in arrays.items()}
    nc = bacc.Bacc("TRN2", target_bir_lowering=False, num_devices=1)
    d = {k: nc.dram_tensor(f"in_{k}", v.shape, F32, kind="ExternalInput").ap() for k, v in arrays.items()}
    d["out"] = nc.dram_tensor("out", (P, KT, SEQ), F32, kind="ExternalOutput").ap()
    for name, shape in (("v_rw", (NT, P, RW)), ("y", (5, P, T)), ("x_mid", (P, KT, T))):
        d[name] = nc.dram_tensor(name, shape, F32).ap()
    build(nc, d)
    r = run_bass_kernel_spmd(nc, [{f"in_{k}": v for k, v in arrays.items()}], core_ids=[0])
    out = r.results[0]["out"]
    return np.ascontiguousarray(np.moveaxis(out, 1, 0).reshape(DM, SEQ).T.reshape(1, SEQ, DM))
```

```python
from contextlib import ExitStack

import numpy as np

import concourse.bass as bass
from concourse import mybir

F32 = mybir.dt.float32
ALU = mybir.AluOpType
ACT = mybir.ActivationFunctionType
AX = mybir.AxisListType
ENGINE = mybir.EngineType

P = 128
DM = 1024
KT = DM // P
CTX, SEQ = 256, 1024
T = CTX + SEQ
DEPTH = 2
HD = 64
RW = 384
PAIRS = RW // P
HEADS = RW // HD
CV = 256
CVT = CV // P
CHUNK = 64
NCH = T // CHUNK
WIN = 128
NT = T // P
QB = SEQ // P
ADA_GROUPS = 4
DECAY = float(np.exp(np.float32(-0.5))) / 2
NORM_EPS, LNX_EPS = 1e-6, 64e-5
MASK_VALUE = -1e30
LEVELS = (2, 4, 8, 16, 32)

N1, N2 = 15, 11
T_CG, T_XIN, T_BG, T_CGATE, T_Q, T_AGATE, T_K, T_KPAD = 0, 2, 4, 6, 8, 11, 14, 15
T_R, T_RK, T_WD, T_AD, T_G = 0, 3, 6, 7, 8
GROUPS = ((0, CTX), (CTX, CTX + 512), (CTX + 512, T))


def table(parts):
    out, at = {}, 0
    for name, n in parts:
        out[name] = at
        at += n
    return out, at


CONST, NCONST = table([
    ("ident", P), ("rot", P), ("headsum", P), ("ones", P), ("headsel", 2), ("reset", 256),
    ("id64", HD), ("strict0", HD), ("arb0", HD), ("akk0", HD), ("ark0", HD), ("first0", HD),
    ("strict1", HD), ("arb1", HD), ("akk1", HD), ("ark1", HD), ("first1", HD), ("join", 5 * HD)])
PARAM, NPARAM = table([
    ("norm_g", KT), ("w0", 2 * PAIRS), ("a0", 2 * PAIRS), ("k_k", PAIRS), ("k_a", PAIRS), ("r_k", PAIRS),
    ("cv_w", 3 * CVT), ("sink", HEADS), ("b_ada", 24)])
DERIV, NDERIV = table([("gs", 2 * KT), ("nsink", HEADS), ("hw0", 2 * PAIRS), ("ha0", 2 * PAIRS), ("hk_a", PAIRS)])


class Signal:

    def __init__(self, ctx, nc, name):
        self.sem, self.base = ctx.enter_context(nc.semaphore(name)), 0

    def at(self, k):
        return k + self.base

    def close(self, total):
        self.base += total


class Order:

    def __init__(self, eng, count):
        self.eng, self.count, self.n, self.off = eng, count, 0, 0

    def __call__(self, ins):
        ins.then_inc(self.count.sem, 1)
        self.n += 1
        return self.n

    def wait(self, n=None):
        self.eng.wait_ge(self.count.sem, (self.n if n is None else n) + self.off + self.count.base)

    def link(self, ins):
        self(ins)
        self.wait()


def build(nc, d):
    with ExitStack() as ctx:
        g = Kernel(nc, ctx, d)
        g.setup()
        for layer in range(DEPTH):
            g.norm(layer)
            g.project_first(layer)
            g.attention(layer)
            g.project_second(layer)
            for way in (0, 1):
                g.decays(layer, way)
                g.scan(layer, way)
            g.readout(layer)
            g.project_out(layer)
        g.final_norm()


class Kernel:
    def __init__(self, nc, ctx, d):
        self.nc, self.ctx, self.d = nc, ctx, d
        self.signals = {}
        self.const = ctx.enter_context(nc.sbuf_tensor("const", [P, NCONST], F32))
        self.param = ctx.enter_context(nc.sbuf_tensor("param", [P, DEPTH, NPARAM], F32))
        self.deriv = ctx.enter_context(nc.sbuf_tensor("deriv", [P, DEPTH, NDERIV], F32))
        self.ada = ctx.enter_context(nc.sbuf_tensor("ada", [P, DEPTH, 24, 2], F32))
        self.fing = ctx.enter_context(nc.sbuf_tensor("fing", [P, KT], F32))
        self.silu = ctx.enter_context(nc.sbuf_tensor("silu", [P, KT, 2], F32))
        self.eps = ctx.enter_context(nc.sbuf_tensor("eps", [P, 2], F32))
        self.tiles = ctx.enter_context(nc.sbuf_tensor("tiles", [P, 16, T], F32))
        self.hid = ctx.enter_context(nc.sbuf_tensor("hid", [P, KT * T], F32))
        self.NEX = 18800
        self.extra = ctx.enter_context(nc.sbuf_tensor("extra", [P, self.NEX], F32))
        self.bank = [ctx.enter_context(nc.psum_tensor(f"bank{i}", [P, 512], F32)) for i in range(8)]

    def sig(self, name):
        if name not in self.signals:
            self.signals[name] = Signal(self.ctx, self.nc, name)
        return self.signals[name]

    def c(self, name, n):
        return self.const[:, CONST[name]:CONST[name] + n]

    def pr(self, layer, name, n, at=0):
        return self.param[:, layer, PARAM[name] + at:PARAM[name] + at + n]

    def dv(self, layer, name, n, at=0):
        return self.deriv[:, layer, DERIV[name] + at:DERIV[name] + at + n]

    def loop(self, engine, start, end):
        return self.nc.Fori(start, end, engines=(engine,))

    @property
    def hT(self):
        return self.hid[:, :].rearrange("p (k t) -> p k t", k=KT)

    def ex(self, at, n):
        assert at + n <= self.NEX
        return self.extra[:, at:at + n]

    def ada_setup(self, batch, slots, rows):
        self.ada_batch, self.ada_slots, self.ada_rows = batch, slots, rows
        self.ada_in = [self.sig(f"w_in{s}") for s in range(2)] + [self.sig(f"y_out{s}") for s in range(2)]
        self.ada_used, self.row_out, self.ada_col, self.ada_done = (
            self.sig(n) for n in ("ada_used", "ada_row_out", "ada_col", "ada_done"))
        self.ada_k = slots[0].shape[1]
        self.ada_pieces = KT // self.ada_k

    def ada_load(self, sp):
        n = len(self.ada_slots)
        for m in range(ADA_GROUPS * self.ada_pieces):
            group, h = divmod(m, self.ada_pieces)
            if m >= n:
                sp.wait_ge(self.ada_used.sem, self.ada_used.at(m - n + 1))
            sp.dma_start(self.ada_slots[m % n], self.d["w_ada"][ADA_GROUPS * self.ada_batch + group]
                         [:, self.ada_k * h:self.ada_k * (h + 1), :]).then_inc(self.ada_in[m % n].sem, 16)

    def ada_multiply(self, pe, group):
        n = len(self.ada_slots)
        if group >= 2:
            pe.wait_ge(self.row_out.sem, self.row_out.at(group - 1))
        for h in range(self.ada_pieces):
            m = group * self.ada_pieces + h
            pe.wait_ge(self.ada_in[m % n].sem, self.ada_in[m % n].at(16 * (m // n) + 16))
            for k in range(self.ada_k):
                kt = h * self.ada_k + k
                ins = pe.matmul(self.bank[6 + group % 2][0:2, :], self.silu[:, kt, :], self.ada_slots[m % n][:, k, :],
                                start=(kt == 0), stop=(kt == KT - 1))
            ins.then_inc(self.ada_used.sem, 1)

    def ada_turn(self, pe, group):
        pe.wait_ge(self.row_out.sem, self.row_out.at(group + 1))
        for n in range(4):
            at = 8 * group + 2 * n
            ins = pe.matmul(self.bank[0][:, at:at + 2], self.ada_rows[0:2, n * P:(n + 1) * P],
                            self.c("ident", 2)[0:2], start=True, stop=True)
        ins.then_inc(self.ada_col.sem, 1)

    def ada_take(self, act, group):
        act.wait_ge(self.ada_used.sem, self.ada_used.at((group + 1) * self.ada_pieces))
        if group:
            act.wait_ge(self.ada_col.sem, self.ada_col.at(group))
        act.copy(self.ada_rows[0:2, :], self.bank[6 + group % 2][0:2, :]).then_inc(self.row_out.sem, 1)

    def ada_finish(self, dve):
        dve.wait_ge(self.ada_col.sem, self.ada_col.at(ADA_GROUPS))
        for q in range(2):
            l, n = divmod(16 * self.ada_batch + 8 * q, 24)
            b = self.pr(l, "b_ada", 8, n).unsqueeze(2).to_broadcast([P, 8, 2])
            dve.tensor_tensor(self.ada[:, l, n:n + 8, :], self.bank[0][:, 16 * q:16 * q + 16].rearrange(
                "p (n s) -> p n s", s=2), b, ALU.add).then_inc(self.ada_done.sem, 1)
            if n == KT:
                dve.wait_ge(self.ada_done.sem, self.ada_done.at(q + 1))
                gs = self.dv(l, "gs", 2 * KT).rearrange("p (k s) -> p k s", s=2)
                ng = self.pr(l, "norm_g", KT).unsqueeze(2).to_broadcast([P, KT, 2])
                dve.scalar_tensor_tensor(out=gs, in0=self.ada[:, l, KT:2 * KT, :], scalar=1.0, in1=ng,
                                         op0=ALU.add, op1=ALU.mult)

    def ada_close(self):
        n, pieces = len(self.ada_slots), ADA_GROUPS * self.ada_pieces
        for s, x in enumerate(self.ada_in[:n]):
            x.close(16 * len(range(s, pieces, n)))
        self.ada_used.close(pieces), self.row_out.close(ADA_GROUPS), self.ada_col.close(ADA_GROUPS)
        self.ada_done.close(2)

    def setup(self):
        nc, d = self.nc, self.d
        loads, silu, small, x_in = (self.sig(n) for n in ("loads", "silu", "order_dve", "x_in"))
        cc = self.ex(0, 2 * KT).rearrange("p (k s) -> p k s", s=2)
        COLS = 512
        rows = self.ex(16, COLS)
        self.ada_setup(0, [self.ex(528 + s * KT * COLS, KT * COLS).rearrange("p (k n) -> p k n", k=KT)
                           for s in range(4)], rows)
        with nc.Block() as block:
            @block.sync
            def _(sp):
                for dst, src in ((self.const[:, :], d["const"]), (self.param[:, :, :], d["param"]),
                                 (self.fing[:, :], d["fing"]), (cc, d["cc"])):
                    sp.dma_start(dst, src).then_inc(loads.sem, 16)
                self.ada_load(sp)
                sp.dma_start(self.tiles[:, 0:KT, :], d["x"]).then_inc(x_in.sem, 16)
                sp.wait_ge(x_in.sem, 16)

            @block.scalar
            def _(act):
                act.wait_ge(loads.sem, 64)
                act.activation(self.silu[:, :, :], cc, ACT.Silu).then_inc(silu.sem, 1)
                for group in range(ADA_GROUPS):
                    self.ada_take(act, group)

            @block.tensor
            def _(pe):
                pe.wait_ge(silu.sem, 1)
                for group in range(ADA_GROUPS):
                    self.ada_multiply(pe, group)
                    self.ada_turn(pe, group)

            @block.vector
            def _(dve):
                o = Order(dve, small)
                dve.wait_ge(loads.sem, 64)
                o(dve.memset(self.eps[:, 0:1], NORM_EPS))
                o(dve.memset(self.eps[:, 1:2], LNX_EPS))
                for l in range(DEPTH):
                    o(dve.tensor_scalar(self.dv(l, "nsink", HEADS), self.pr(l, "sink", HEADS), -1.0, None, ALU.mult))
                    o(dve.tensor_scalar(self.dv(l, "hw0", 6), self.pr(l, "w0", 6), 0.5, None, ALU.mult))
                    o(dve.tensor_scalar(self.dv(l, "ha0", 6), self.pr(l, "a0", 6), 0.5, None, ALU.mult))
                    o(dve.tensor_scalar(self.dv(l, "hk_a", 3), self.pr(l, "k_a", 3), 0.5, None, ALU.mult))
                self.ada_finish(dve)
                self.total_order = o.n
        small.close(self.total_order)
        loads.close(64), x_in.close(16), silu.close(1)
        self.ada_close()

    def inv_rms(self, block, x, sq, rstd, lo, groups, then=None):
        squares, sums, roots = (self.sig(n) for n in ("squares", "sums", "roots"))
        pairs = self.sig("pairs")

        @block.scalar
        def _(act):
            for k in range(KT):
                if k >= 4:
                    act.wait_ge(sums.sem, sums.at(k // 2 - 1))
                act.activation(sq[:, k % 4, lo:T], x[:, k, lo:T], ACT.Square).then_inc(squares.sem, 1)
            act.wait_ge(sums.sem, sums.at(KT // 2))
            for n, (a, b) in enumerate(groups):
                act.activation(rstd[:, a:b], self.bank[n][:, 0:b - a], ACT.Sqrt, scale=1.0 / DM,
                               bias=self.eps[:, 0:1]).then_inc(roots.sem, 1)
            if then:
                then(act)

        @block.tensor
        def _(pe):
            for m in range(KT // 2):
                pe.wait_ge(pairs.sem, pairs.at(m + 1))
                for n, (a, b) in enumerate(groups):
                    ins = pe.matmul(self.bank[n][:, 0:b - a], self.c("ones", P), sq[:, 2 * (m % 2), a:b],
                                    start=(m == 0), stop=(m == KT // 2 - 1))
                ins.then_inc(sums.sem, 1)

        def add_pairs(dve):
            for m in range(KT // 2):
                dve.wait_ge(squares.sem, squares.at(2 * m + 2))
                at = 2 * (m % 2)
                dve.tensor_tensor(sq[:, at, lo:T], sq[:, at, lo:T], sq[:, at + 1, lo:T], ALU.add).then_inc(pairs.sem, 1)
        return add_pairs

    def norm(self, layer):
        nc = self.nc
        sq = self.ex(0, 4 * T).rearrange("p (s t) -> p s t", s=4)
        rstd = self.ex(4 * T, T)
        h, x = self.hT, self.tiles[:, 0:KT, :]
        roots, order = self.sig("roots"), self.sig("order_dve")
        gs = self.dv(layer, "gs", 2 * KT).rearrange("p (k s) -> p k s", s=2)
        normed, shifted = self.sig("normed"), self.sig("shifted")

        def affine(act):
            for k in range(KT):
                act.wait_ge(normed.sem, normed.at(k + 1))
                for s, (a, b) in ((1, (0, CTX)), (0, (CTX, T))):
                    act.activation(h[:, k, a:b], h[:, k, a:b], ACT.Identity, scale=gs[:, k, s:s + 1],
                                   bias=self.ada[:, layer, k, s:s + 1]).then_inc(shifted.sem, 1)
        with nc.Block() as block:
            add_pairs = self.inv_rms(block, x, sq, rstd, 0, GROUPS, affine)

            @block.vector
            def _(dve):
                o = Order(dve, order)
                add_pairs(dve)
                for n, (a, b) in enumerate(GROUPS):
                    dve.wait_ge(roots.sem, roots.at(n + 1))
                    o(dve.reciprocal(rstd[:, a:b], rstd[:, a:b]))
                o.wait()
                for k in range(KT):
                    dve.tensor_tensor(h[:, k, :], x[:, k, :], rstd, ALU.mult).then_inc(normed.sem, 1)
                self.total_order = o.n
        self.sig("squares").close(KT), self.sig("sums").close(KT // 2), self.sig("pairs").close(KT // 2), roots.close(len(GROUPS))
        normed.close(KT), shifted.close(2 * KT), order.close(self.total_order)

    def stream_sync(self, sp, w, n, ring, ng):
        w_in, ready = [self.sig(f"w_in{s}") for s in range(2)], self.sig("acc_ready")

        def load(s, t):
            sp.dma_start(ring[s], w[bass.ds(t, 1)].rearrange("a p k n -> (a p) k n")).then_inc(w_in[s].sem, 16)
        for s in range(2):
            load(s, s)
        with self.loop(ENGINE.SP, 1, n // 2) as i:
            for s in range(2):
                sp.wait_ge(ready.sem, ng * (2 * i + s - 1) + ready.base)
                load(s, 2 * i + s)
        if n % 2:
            sp.wait_ge(ready.sem, ready.at(ng * (n - 2)))
            load(0, n - 1)

    def stream_pe(self, pe, rhs, n, ring, groups, last_groups):
        ready, free = self.sig("acc_ready"), self.sig("acc_free")
        w_in = [self.sig(f"w_in{s}") for s in range(2)]
        ng = len(groups)

        def tile(s, i, gs, skip):
            t = 2 * i + s
            pe.wait_ge(w_in[s].sem, 16 * i + 16 + w_in[s].base)
            for q, (a, b) in enumerate(gs):
                if not skip:
                    pe.wait_ge(free.sem, ng * t + (q + 1 - 2 * ng) + free.base)
                for k in range(KT):
                    ins = pe.matmul(self.bank[3 * s + q][:, 0:b - a], ring[s][:, k, :], rhs[:, k, a:b],
                                    start=(k == 0), stop=(k == KT - 1))
                ins.then_inc(ready.sem, 1)
        for s in range(2):
            tile(s, 0, groups, True)
        with self.loop(ENGINE.PE, 1, n // 2) as i:
            for s in range(2):
                tile(s, i, groups, False)
        if n % 2:
            pe.wait_ge(free.sem, free.at(ng * (n - 1)))
            tile(0, n // 2, last_groups, True)

    def stream_act(self, act, out, n, groups, last_groups, func=ACT.Copy):
        ready, free = self.sig("acc_ready"), self.sig("acc_free")
        ng = len(groups)

        def tile(s, t, gs):
            for q, (a, b) in enumerate(gs):
                act.wait_ge(ready.sem, ng * t + q + 1 + ready.base)
                act.activation(out[:, bass.ds(t, 1), a:b], self.bank[3 * s + q][:, 0:b - a].unsqueeze(1),
                               func).then_inc(free.sem, 1)
        with self.loop(ENGINE.Activation, 0, n // 2) as i:
            for s in range(2):
                tile(s, 2 * i + s, groups)
        if n % 2:
            tile(0, n - 1, last_groups)
        self.counts = ng * (n - n % 2) + len(last_groups) * (n % 2)

    def stream_close(self, n, total):
        self.sig("w_in0").close(16 * (n - n // 2)), self.sig("w_in1").close(16 * (n // 2))
        self.sig("acc_ready").close(total), self.sig("acc_free").close(total)

    def project_first(self, layer):
        nc, d = self.nc, self.d
        keep = layer < DEPTH - 1
        groups = GROUPS if keep else GROUPS[1:]
        lo = 0 if keep else CTX
        tiles = self.tiles
        order = self.sig("order_dve")
        free, gate, wv_in, v_ready, v_taken, v_out, trig = (
            self.sig(n) for n in ("acc_free", "gates", "wv_in", "v_ready", "v_taken", "dma_out", "trig_in"))
        rot_ready, rot_used, rope, conv_done = (self.sig(n) for n in ("rot_ready", "rot_used", "rope", "conv_done"))
        at = 0

        def take(n):
            nonlocal at
            at += n
            return self.ex(at - n, n)
        UW = T + 4
        u = take(CVT * UW).rearrange("p (i t) -> p i t", i=CVT)
        cvt = take(CVT * T).rearrange("p (i t) -> p i t", i=CVT)
        v_rw = take(NT * RW).rearrange("p (n v) -> p n v", n=NT)
        ring = [take(DM).rearrange("p (k n) -> p k n", k=KT) for _ in range(2)]
        wv = take(KT * 512).rearrange("p (k n) -> p k n", k=KT)
        assert at <= 15200
        v_at = self.v_at = self.ex(15200, (NT + 2) * P).rearrange("p (n v) -> p n v", n=NT + 2)
        trigt = self.ex(16736, 2 * SEQ).rearrange("p (s t) -> p s t", s=2)
        kpad = tiles[:, T_KPAD, :]
        rope_tiles = (T_Q, T_Q + 1, T_Q + 2, T_K)
        loops = N1 - 1
        stream = len(groups) * loops + 3
        with nc.Block() as block:
            @block.sync
            def _(sp):
                sp.dma_start(trigt, d["trig"]).then_inc(trig.sem, 16)
                sp.dma_start(wv, d["w_v"][layer]).then_inc(wv_in.sem, 16)
                self.stream_sync(sp, d["w_1"][layer], N1, ring, len(groups))
                sp.wait_ge(v_taken.sem, v_taken.at(2 * NT))
                sp.dma_start(d["v_rw"].rearrange("n p v -> p n v"), v_rw).then_inc(v_out.sem, 16)
                sp.wait_ge(conv_done.sem, conv_done.at(CVT))
                for i in range(CVT):
                    sp.dma_start(d["y"][PAIRS + i, :, lo:T], cvt[:, i, lo:T]).then_inc(v_out.sem, 16)
                sp.wait_ge(v_out.sem, v_out.at(16 + 16 * CVT))

            @block.tensor
            def _(pe):
                self.stream_pe(pe, self.hT, N1, ring, groups, GROUPS)
                pe.wait_ge(wv_in.sem, wv_in.at(16))
                for n in range(NT):
                    if n >= 2:
                        pe.wait_ge(v_taken.sem, v_taken.at(2 * n - 2))
                    for k in range(KT):
                        ins = pe.matmul(self.bank[6 + n % 2][:, :], self.hT[:, k, n * P:(n + 1) * P], wv[:, k, :],
                                        start=(k == 0), stop=(k == KT - 1))
                    ins.then_inc(v_ready.sem, 1)
                pe.wait_ge(free.sem, free.at(stream))
                pe.wait_ge(v_taken.sem, v_taken.at(2 * NT))
                for m in range(8):
                    t, (a, b) = rope_tiles[m // 2], GROUPS[1 + m % 2]
                    if m >= 2:
                        pe.wait_ge(rot_used.sem, rot_used.at(m - 1))
                    pe.matmul(self.bank[6 + m % 2][:, :], self.c("rot", P), tiles[:, t, a:b],
                              start=True, stop=True).then_inc(rot_ready.sem, 1)

            @block.scalar
            def _(act):
                self.stream_act(act, tiles, N1, groups, GROUPS)
                act.wait_ge(free.sem, free.at(stream))
                for t, n in ((T_CGATE, CVT), (T_AGATE, PAIRS)):
                    act.activation(tiles[:, t:t + n, lo:T], tiles[:, t:t + n, lo:T], ACT.Silu).then_inc(gate.sem, 1)
                for n in range(NT):
                    act.wait_ge(v_ready.sem, v_ready.at(n + 1))
                    act.copy(v_rw[:, n, :], self.bank[6 + n % 2][:, 0:RW]).then_inc(v_taken.sem, 1)
                    slot = n if n < 2 else n + 1
                    act.copy(v_at[:, slot, :], self.bank[6 + n % 2][:, RW:512]).then_inc(v_taken.sem, 1)

            @block.vector
            def _(dve):
                o = Order(dve, order)
                o(dve.memset(v_at[:, 2, :], 0.0))
                o(dve.memset(v_at[:, NT + 1, :], 0.0))
                for z in (0, CTX + 1, CTX + 2, T + 3):
                    o(dve.memset(u[:, :, z:z + 1], 0.0))
                o(dve.memset(kpad[:, 0:P], 0.0))
                o(dve.memset(kpad[:, P + SEQ:T], 0.0))
                dve.wait_ge(free.sem, free.at(4 * len(groups)))
                spans = [(0, CTX, 1), (CTX, T, 3)] if keep else [(CTX, T, 3)]
                for a, b, s in spans:
                    o(dve.tensor_tensor(u[:, :, a + s:b + s], tiles[:, T_CG:T_CG + CVT, a:b],
                                        tiles[:, T_XIN:T_XIN + CVT, a:b], ALU.mult))
                o.wait()
                w = self.pr(layer, "cv_w", 3 * CVT).rearrange("p (j i) -> p j i", j=3)
                for j in range(3):
                    for a, b, s in spans:
                        for i in range(CVT):
                            src = u[:, i, a + s + j - 1:b + s + j - 1]
                            if j == 0:
                                o(dve.tensor_scalar(cvt[:, i, a:b], src, w[:, j, i:i + 1], None, ALU.mult))
                            else:
                                o(dve.scalar_tensor_tensor(out=cvt[:, i, a:b], in0=src, scalar=w[:, j, i:i + 1],
                                                           in1=cvt[:, i, a:b], op0=ALU.mult, op1=ALU.add))
                    o.wait()
                dve.wait_ge(free.sem, free.at(6 * len(groups)))
                o.link(dve.tensor_tensor(cvt[:, :, lo:T], cvt[:, :, lo:T], tiles[:, T_BG:T_BG + CVT, lo:T], ALU.mult))
                dve.wait_ge(gate.sem, gate.at(1))
                for i in range(CVT):
                    dve.tensor_tensor(cvt[:, i, lo:T], cvt[:, i, lo:T], tiles[:, T_CGATE + i, lo:T],
                                      ALU.mult).then_inc(conv_done.sem, 1)
                dve.wait_ge(trig.sem, trig.at(16))
                for m in range(8):
                    t, (a, b) = rope_tiles[m // 2], GROUPS[1 + m % 2]
                    cos, sin = trigt[:, 0, a - CTX:b - CTX], trigt[:, 1, a - CTX:b - CTX]
                    part = u[:, m % 2, 0:512]
                    dst = tiles[:, t, a:b] if t != T_K else kpad[:, P + a - CTX:P + b - CTX]
                    dve.wait_ge(rot_ready.sem, rot_ready.at(m + 1))
                    dve.tensor_tensor(part, self.bank[6 + m % 2][:, :], sin, ALU.mult).then_inc(rot_used.sem, 1)
                    o(dve.tensor_tensor(dst, tiles[:, t, a:b], cos, ALU.mult))
                    o.wait()
                    dve.wait_ge(rot_used.sem, rot_used.at(m + 1))
                    dve.tensor_tensor(dst, dst, part, ALU.add).then_inc(rope.sem, 1)
                self.total_order = o.n
        order.close(self.total_order)
        self.stream_close(N1, stream)
        gate.close(2), wv_in.close(16), v_ready.close(NT), v_taken.close(2 * NT), v_out.close(16 + 16 * CVT)
        trig.close(16), rot_ready.close(8), rot_used.close(8), rope.close(8), conv_done.close(CVT)

    def attention(self, layer):
        nc, d = self.nc, self.d
        tiles, v_at, bank = self.tiles, self.v_at, self.bank
        strips_in, staged, scores, masked, center, nmax, probs, esink, pt, pt_d, pt_a, o_ready, o_used, inv, \
            yt_ready, yt_used = (self.sig(n) for n in (
                "strips_in", "staged", "scores", "masked", "center", "nmax", "probs", "esink", "pt", "pt_d", "pt_a",
                "o_ready", "o_used", "inv", "yt_ready", "yt_used"))
        y_out = [self.sig(f"y_out{s}") for s in range(2)]
        order = self.sig("order_dve")
        at = 0

        def take(n):
            nonlocal at
            at += n
            return self.ex(at - n, n)
        strips = take(2 * QB * P).rearrange("p (s n) -> p s n", s=2)
        qs = [take(HEADS * P).rearrange("p (q j t) -> p q j t", q=2, j=PAIRS) for _ in range(2)]
        ks = [take(3 * P) for _ in range(2)]
        vs = [take(3 * P).rearrange("p (n v) -> p n v", n=3) for _ in range(2)]
        sm = [take(5 * P) for _ in range(2)]
        ptt = [take(5 * P).rearrange("p (n q) -> p n q", n=5) for _ in range(2)]
        rmax, nm, den, es, rden = (take(HEADS) for _ in range(5))
        yn = [take(RW).rearrange("p (h v) -> p h v", h=HEADS) for _ in range(2)]
        yg, *yo = (take(RW).rearrange("p (j t) -> p j t", j=PAIRS) for _ in range(3))
        assert at <= 15200
        kpad, kctx = tiles[:, T_KPAD, :], tiles[:, T_K, 0:CTX]
        obank = bank[6][:, 0:RW].rearrange("p (j t) -> p j t", j=PAIRS)
        tbank = bank[7][:, 0:RW].rearrange("p (j t) -> p j t", j=PAIRS)
        nsink, sink = self.dv(layer, "nsink", HEADS), self.pr(layer, "sink", HEADS)
        keep = layer < DEPTH - 1
        CB = CTX // P if keep else 0
        blocks = CB + QB

        def run(engine, body):
            if keep:
                for s in range(2):
                    body(s, 0, s, s, False, True)
                with self.loop(engine, 0, QB // 2) as i:
                    for s in range(2):
                        body(s, i + 1, 2 * i + s + CB, 2 * i + s, True, False)
            else:
                for s in range(2):
                    body(s, 0, s, s, True, True)
                with self.loop(engine, 1, QB // 2) as i:
                    for s in range(2):
                        body(s, i, 2 * i + s, 2 * i + s, True, False)

        def cols(b, windowed):
            return b * P + (CTX if windowed else 0)
        HP = [(n % 2, n // 2) for n in range(HEADS)]

        with nc.Block() as block:
            @block.sync
            def _(sp):
                sp.dma_start(strips, d["strips"]).then_inc(strips_in.sem, 16)

                def body(s, i, u, b, windowed, first):
                    sp.wait_ge(yt_used.sem, u + 1 + yt_used.base)
                    sp.dma_start(d["y"][0:PAIRS, :, bass.ds(cols(b, windowed), P)].rearrange("j p t -> p j t"),
                                 yo[s]).then_inc(y_out[s].sem, 16)
                run(ENGINE.SP, body)
                for x in y_out:
                    sp.wait_ge(x.sem, x.at(8 * blocks))

            @block.gpsimd
            def _(pool):
                def body(s, i, u, b, windowed, first):
                    if not first:
                        pool.wait_ge(o_ready.sem, HEADS * (u - 1) + o_ready.base)
                    q = tiles[:, T_Q:T_Q + PAIRS, bass.ds(cols(b, windowed), P)]
                    for p in range(2):
                        pool.tensor_tensor(qs[s][:, p], q, self.c("headsel", 2)[:, p:p + 1].unsqueeze(2).to_broadcast(
                            [P, PAIRS, P]), ALU.mult).then_inc(staged.sem, 1)
                    if windowed:
                        pool.tensor_copy(ks[s], kpad[:, bass.ds(b * P, 3 * P)]).then_inc(staged.sem, 1)
                        pool.tensor_copy(vs[s], v_at[:, bass.ds(b + 2, 3), :]).then_inc(staged.sem, 1)
                    else:
                        pool.tensor_copy(ks[s][:, 0:1], kctx[:, 0:1]).then_inc(staged.sem, 1)
                        pool.tensor_copy(vs[s][:, 0, 0:1], v_at[:, 0, 0:1]).then_inc(staged.sem, 1)
                run(ENGINE.Pool, body)

            @block.tensor
            def _(pe):
                def body(s, i, u, b, windowed, first):
                    def score(n):
                        p, j = HP[n]
                        if n >= 2 or not (first and s == 0):
                            pe.wait_ge(masked.sem, HEADS * u + (n - 1) + masked.base)
                            pe.wait_ge(center.sem, 2 * (HEADS * u + (n - 1)) + center.base)
                        q = qs[s][:, p, j, :]
                        if windowed:
                            pe.matmul(bank[2 * p][:, 0:3 * P], q, ks[s], start=True, stop=True)
                        pe.matmul(bank[2 * p][:, 3 * P:4 * P], q, kctx[:, 0:P], start=True, stop=True)
                        pe.matmul(bank[2 * p + 1][:, 0:P], q, kctx[:, P:2 * P], start=True,
                                  stop=True).then_inc(scores.sem, 1)

                    def turn(n):
                        if n > 0 or not (first and s == 0):
                            pe.wait_ge(pt_d.sem, HEADS * u + n + pt_d.base)
                            pe.wait_ge(pt_a.sem, HEADS * u + n + pt_a.base)
                        pe.wait_ge(probs.sem, HEADS * u + n + 1 + probs.base)
                        for k in range(0 if windowed else 3, 4):
                            pe.transpose(bank[4][:, k * P:(k + 1) * P], sm[n % 2][:, k * P:(k + 1) * P],
                                         self.c("ident", P))
                        pe.transpose(bank[5][:, 0:P], sm[n % 2][:, 4 * P:5 * P],
                                     self.c("ident", P)).then_inc(pt.sem, 1)

                    def mix(n):
                        p, j = HP[n]
                        pe.wait_ge(pt_d.sem, HEADS * u + n + 1 + pt_d.base)
                        pe.wait_ge(pt_a.sem, HEADS * u + n + 1 + pt_a.base)
                        if n == 0 and not (first and s == 0):
                            pe.wait_ge(o_used.sem, u + o_used.base)
                        cv = slice(HD * p, HD * p + HD)
                        own = [(k, vs[s][:, k, cv]) for k in range(3)] if windowed else []
                        own += [(3 + k, v_at[:, k, cv]) for k in range(2)]
                        for m, (k, v) in enumerate(own):
                            ins = pe.matmul(obank[cv, j, :], v, ptt[n % 2][:, k, :],
                                            start=(m == 0), stop=(m == len(own) - 1))
                        ins.then_inc(o_ready.sem, 1)
                    pe.wait_ge(staged.sem, 4 * u + 4 + staged.base)
                    score(0)
                    score(1)
                    for n in range(HEADS):
                        turn(n)
                        if n + 2 < HEADS:
                            score(n + 2)
                        if n == HEADS - 1:
                            pe.wait_ge(inv.sem, 3 * u + 3 + inv.base)
                            if not (first and s == 0):
                                pe.wait_ge(yt_used.sem, u + yt_used.base)
                            for j in range(PAIRS):
                                ins = pe.transpose(tbank[:, j, :],
                                                   yn[s][:, 2 * j:2 * j + 2, :].rearrange("p h v -> p (h v)"),
                                                   self.c("ident", P))
                            ins.then_inc(yt_ready.sem, 1)
                        mix(n)
                run(ENGINE.PE, body)

            @block.scalar
            def _(act):
                def body(s, i, u, b, windowed, first):
                    def out_of_psum(n):
                        p, j = HP[n]
                        h = sm[n % 2]
                        act.wait_ge(scores.sem, HEADS * u + n + 1 + scores.base)
                        if n >= 2 or not (first and s == 0):
                            act.wait_ge(pt.sem, HEADS * u + (n - 1) + pt.base)
                        act.copy(h[:, 4 * P:5 * P], bank[2 * p + 1][:, 0:P]).then_inc(center.sem, 1)
                        act.wait_ge(masked.sem, HEADS * u + n + 1 + masked.base)
                        if windowed:
                            act.copy(h[:, 0:4 * P].rearrange("p (c x) -> p c x", x=2 * P)[:, :, P:2 * P],
                                     bank[2 * p][:, :].rearrange("p (c x) -> p c x", x=2 * P)[:, :, P:2 * P]
                                     ).then_inc(center.sem, 1)
                        else:
                            act.copy(h[:, 3 * P:4 * P], bank[2 * p][:, 3 * P:4 * P]).then_inc(center.sem, 1)

                    def exps(n):
                        p, j = HP[n]
                        lo = 0 if windowed else 3 * P
                        h = sm[n % 2][:, lo:5 * P]
                        act.wait_ge(nmax.sem, HEADS * u + n + 1 + nmax.base)
                        if n == 0 and not (first and s == 0):
                            act.wait_ge(inv.sem, 3 * u + inv.base)
                        act.activation(h, h, ACT.Exp, scale=HD ** -0.5, bias=nm[:, 2 * j + p:2 * j + p + 1],
                                       accum_out=den[:, 2 * j + p:2 * j + p + 1]).then_inc(probs.sem, 1)
                        act.activation(es[:, 2 * j + p:2 * j + p + 1], sink[:, 2 * j + p:2 * j + p + 1], ACT.Exp,
                                       bias=nm[:, 2 * j + p:2 * j + p + 1]).then_inc(esink.sem, 1)

                    def pt_copy(n):
                        act.wait_ge(pt.sem, HEADS * u + n + 1 + pt.base)
                        act.copy(ptt[n % 2][:, 4, :], bank[5][:, 0:P]).then_inc(pt_a.sem, 1)
                    out_of_psum(0)
                    for n in range(HEADS):
                        exps(n)
                        if n + 1 < HEADS:
                            out_of_psum(n + 1)
                        pt_copy(n)
                run(ENGINE.Activation, body)

            @block.vector
            def _(dve):
                dve.wait_ge(strips_in.sem, strips_in.at(16))

                def body(s, i, u, b, windowed, first):
                    def mask(n):
                        p, j = HP[n]
                        h = sm[n % 2]
                        lo = 0 if windowed else 3 * P
                        hn = slice(2 * j + p, 2 * j + p + 1)
                        dve.wait_ge(scores.sem, HEADS * u + n + 1 + scores.base)
                        if n >= 2 or not (first and s == 0):
                            dve.wait_ge(pt.sem, HEADS * u + (n - 1) + pt.base)
                        if windowed:
                            dve.tensor_tensor(h[:, 0:4 * P].rearrange("p (c x) -> p c x", x=2 * P)[:, :, 0:P],
                                              bank[2 * p][:, :].rearrange("p (c x) -> p c x", x=2 * P)[:, :, 0:P],
                                              strips[:, :, bass.ds(b * P, P)], ALU.add).then_inc(masked.sem, 1)
                        else:
                            dve.tensor_copy(h[:, 0:1], nsink[:, 0:1]).then_inc(masked.sem, 1)
                        dve.wait_ge(masked.sem, HEADS * u + n + 1 + masked.base)
                        dve.wait_ge(center.sem, 2 * (HEADS * u + n + 1) + center.base)
                        dve.reduce_max(rmax[:, hn], h[:, lo:5 * P], AX.X).then_inc(order.sem, 1)
                        dve.wait_ge(order.sem, HEADS * u + n + 1 + order.base)
                        dve.scalar_tensor_tensor(out=nm[:, hn], in0=rmax[:, hn], scalar=-HD ** -0.5, in1=nsink[:, hn],
                                                 op0=ALU.mult, op1=ALU.min).then_inc(nmax.sem, 1)

                    def pt_copy(n):
                        lo = 0 if windowed else 3
                        dve.wait_ge(pt.sem, HEADS * u + n + 1 + pt.base)
                        if n >= 2 or not (first and s == 0):
                            dve.wait_ge(o_ready.sem, HEADS * u + (n - 1) + o_ready.base)
                        dve.tensor_copy(ptt[n % 2][:, lo:4, :], bank[4][:, lo * P:4 * P].rearrange(
                            "p (n q) -> p n q", q=P)).then_inc(pt_d.sem, 1)
                    def invert():
                        dve.wait_ge(esink.sem, HEADS * u + HEADS + esink.base)
                        dve.wait_ge(probs.sem, HEADS * u + HEADS + probs.base)
                        dve.tensor_tensor(rden, den, es, ALU.add).then_inc(inv.sem, 1)
                        dve.wait_ge(inv.sem, 3 * u + 1 + inv.base)
                        dve.reciprocal(rden, rden).then_inc(inv.sem, 1)
                        dve.wait_ge(inv.sem, 3 * u + 2 + inv.base)
                        dve.tensor_copy(yn[s], rden.unsqueeze(2).to_broadcast([P, HEADS, HD])).then_inc(inv.sem, 1)
                    mask(0)
                    for n in range(HEADS):
                        if n + 1 < HEADS:
                            mask(n + 1)
                        else:
                            invert()
                        pt_copy(n)
                    dve.wait_ge(o_ready.sem, HEADS * u + HEADS + o_ready.base)
                    dve.tensor_tensor(yg, obank, tiles[:, T_AGATE:T_AGATE + PAIRS, bass.ds(cols(b, windowed), P)],
                                      ALU.mult).then_inc(o_used.sem, 1)
                    dve.wait_ge(o_used.sem, u + 1 + o_used.base)
                    dve.wait_ge(yt_ready.sem, u + 1 + yt_ready.base)
                    if not first:
                        dve.wait_ge(y_out[s].sem, 16 * i + y_out[s].base)
                    dve.tensor_tensor(yo[s], yg, tbank, ALU.mult).then_inc(yt_used.sem, 1)
                run(ENGINE.DVE, body)
        strips_in.close(16), staged.close(4 * blocks), inv.close(3 * blocks)
        for x in y_out:
            x.close(8 * blocks)
        for x in (scores, masked, nmax, probs, esink, pt, pt_d, pt_a, o_ready, order):
            x.close(HEADS * blocks)
        center.close(2 * HEADS * blocks)
        for x in (o_used, yt_ready, yt_used):
            x.close(blocks)

    def project_second(self, layer):
        nc, d, tiles = self.nc, self.d, self.tiles
        keep = layer < DEPTH - 1
        free, gate, order = (self.sig(n) for n in ("acc_free", "gates", "order_dve"))
        ksq, ksum, kmax, kroot, bonus_in, bonus_ready = (
            self.sig(n) for n in ("ksq", "ksum", "kmax", "kroot", "bonus_in", "bonus_ready"))
        kk = self.kk = self.ex(0, PAIRS * T).rearrange("p (j t) -> p j t", j=PAIRS)
        rk = self.ex(3840, PAIRS * T).rearrange("p (j t) -> p j t", j=PAIRS)
        norm = self.ex(7680, PAIRS * T).rearrange("p (j t) -> p j t", j=PAIRS)
        sq = self.ex(11520, PAIRS * T).rearrange("p (j t) -> p j t", j=PAIRS)
        ring = [self.ex(15360 + s * DM, DM).rearrange("p (k n) -> p k n", k=KT) for s in range(2)]
        self.bonus = self.ex(17408, NT * HEADS).rearrange("p (n h) -> p n h", h=HEADS)
        stream = 3 * (N2 - 1) + len(GROUPS)
        bbank = bank = self.bank[7][:, 0:NT * HEADS].rearrange("p (n h) -> p n h", h=HEADS)
        with nc.Block() as block:
            @block.sync
            def _(sp):
                self.stream_sync(sp, d["w_2"][layer], N2, ring, 3)

            @block.tensor
            def _(pe):
                self.stream_pe(pe, self.hT, N2, ring, GROUPS, GROUPS)
                for j in range(PAIRS):
                    pe.wait_ge(ksq.sem, ksq.at(j + 1))
                    for q, (a, b) in enumerate(GROUPS):
                        m = 3 * j + q
                        if m < 3:
                            pe.wait_ge(free.sem, free.at(stream))
                        else:
                            pe.wait_ge(kroot.sem, kroot.at(m - 2))
                        pe.matmul(self.bank[m % 3][:, 0:b - a], self.c("headsum", P), sq[:, j, a:b],
                                  start=True, stop=True).then_inc(ksum.sem, 1)
                pe.wait_ge(bonus_in.sem, bonus_in.at(1))
                for n in range(NT):
                    for j in range(PAIRS):
                        ins = pe.matmul(bbank[:, n, 2 * j:2 * j + 2], rk[:, j, n * P:(n + 1) * P],
                                        self.c("headsel", 2), start=True, stop=True)
                ins.then_inc(bonus_ready.sem, 1)

            @block.scalar
            def _(act):
                self.stream_act(act, tiles, N2, GROUPS, GROUPS)
                act.wait_ge(free.sem, free.at(stream))
                act.activation(tiles[:, T_WD, :], tiles[:, T_WD, :], ACT.Tanh).then_inc(gate.sem, 1)
                act.activation(tiles[:, T_G:T_G + PAIRS, :], tiles[:, T_G:T_G + PAIRS, :], ACT.Silu).then_inc(gate.sem, 1)
                for j in range(PAIRS):
                    for q, (a, b) in enumerate(GROUPS):
                        m = 3 * j + q
                        act.wait_ge(ksum.sem, ksum.at(m + 1))
                        act.activation(norm[:, j, a:b], self.bank[m % 3][:, 0:b - a], ACT.Copy).then_inc(kroot.sem, 1)
                act.wait_ge(kmax.sem, kmax.at(1))
                act.activation(norm, norm, ACT.Sqrt).then_inc(kroot.sem, 1)

            @block.vector
            def _(dve):
                o = Order(dve, order)
                k, r = tiles[:, T_RK:T_RK + PAIRS, :], tiles[:, T_R:T_R + PAIRS, :]
                dve.wait_ge(free.sem, free.at(18))
                for j in range(PAIRS):
                    o.link(dve.tensor_scalar(kk[:, j, :], k[:, j, :], self.pr(layer, "k_k", 1, j), None, ALU.mult))
                    dve.tensor_tensor(sq[:, j, :], kk[:, j, :], kk[:, j, :], ALU.mult).then_inc(ksq.sem, 1)
                for j in range(PAIRS):
                    o(dve.tensor_scalar(rk[:, j, :], r[:, j, :], self.pr(layer, "r_k", 1, j), None, ALU.mult))
                o.wait()
                dve.tensor_tensor(rk, rk, k, ALU.mult).then_inc(bonus_in.sem, 1)
                dve.wait_ge(kroot.sem, kroot.at(9))
                dve.tensor_scalar(norm, norm, 1e-12, None, ALU.max).then_inc(kmax.sem, 1)
                dve.wait_ge(kroot.sem, kroot.at(10))
                o.link(dve.reciprocal(norm, norm))
                o.link(dve.tensor_tensor(kk, kk, norm, ALU.mult))
                dve.wait_ge(bonus_ready.sem, bonus_ready.at(1))
                o.link(dve.tensor_copy(self.bonus, bbank))
                self.total_order = o.n
        order.close(self.total_order)
        self.stream_close(N2, stream)
        gate.close(2), ksq.close(3), ksum.close(9), kmax.close(1), kroot.close(10)
        bonus_in.close(1), bonus_ready.close(1)

    def decays(self, layer, way):
        nc, tiles = self.nc, self.tiles
        lo_in, lo_used, cum, ends, ones_col, order, done = (self.sig(n) for n in (
            "lora_ready", "lora_used", "cumulated", "exps", "ones_col", "order_dve", "scaled"))
        self.EP = self.ex(3840, PAIRS * NCH * 65).rearrange("p (j c t) -> p j c t", j=PAIRS, c=NCH)
        self.Bs = self.ex(7740, PAIRS * T).rearrange("p (j t) -> p j t", j=PAIRS)
        self.Ks = self.ex(11580, PAIRS * T).rearrange("p (j t) -> p j t", j=PAIRS)
        off, unit = (1, 0) if way == 0 else (0, CHUNK)
        th = tiles[:, 11:11 + PAIRS, :]
        ta = self.hid[:, 0:PAIRS * T].rearrange("p (j t) -> p j t", j=PAIRS)
        en = self.hid[:, 3840:3840 + 2 * T].rearrange("p (s t) -> p s t", s=2)
        lora = tiles[:, 14, 0:2 * RW].rearrange("p (s v) -> p s v", s=2)
        lora_in = self.sig("lora_in")
        rows = slice(HD * way, HD * way + HD)
        others = slice(HD - HD * way, P - HD * way)
        EP, Bs, Ks, kk = self.EP, self.Bs, self.Ks, self.kk
        ada = layer == 0
        if ada:
            slots = [self.ex(at, 2 * 512) for at in (15480, 17472)] + [tiles[:, 15, 0:2 * 512]]
            self.ada_setup(1 + way, [x.rearrange("p (k n) -> p k n", k=2) for x in slots], tiles[:, 14, 2 * RW:T])
        with nc.Block() as block:
            @block.sync
            def _(sp):
                sp.dma_start(lora[rows], self.d["lora"][layer][rows]).then_inc(lora_in.sem, 16)
                if ada:
                    self.ada_load(sp)

            @block.tensor
            def _(pe):
                pe.wait_ge(lora_in.sem, lora_in.at(16))
                pe.wait_ge(ones_col.sem, ones_col.at(2))
                for j in range(PAIRS):
                    for s, src in ((0, T_WD), (1, T_AD)):
                        for q, (a, b) in enumerate(GROUPS):
                            if j > 0:
                                pe.wait_ge(lo_used.sem, lo_used.at(6 * (j - 1) + 3 * s + q + 1))
                            pe.matmul(self.bank[3 * s + q][:, 0:b - a], lora[:, s, j * P:(j + 1) * P],
                                      tiles[:, src, a:b], start=True, stop=True).then_inc(lo_in.sem, 1)
                if ada:
                    pe.wait_ge(lo_used.sem, lo_used.at(18))
                    self.ada_multiply(pe, 0)
                    for group in range(1, ADA_GROUPS):
                        self.ada_multiply(pe, group)
                        self.ada_turn(pe, group - 1)
                    self.ada_turn(pe, ADA_GROUPS - 1)

            @block.scalar
            def _(act):
                for j in range(PAIRS):
                    for s, dst, bias in ((0, th, "hw0"), (1, ta, "ha0")):
                        for q, (a, b) in enumerate(GROUPS):
                            act.wait_ge(lo_in.sem, lo_in.at(6 * j + 3 * s + q + 1))
                            act.activation(dst[:, j, a:b], self.bank[3 * s + q][:, 0:b - a], ACT.Tanh, scale=0.5,
                                           bias=self.dv(layer, bias, 1, PAIRS * way + j)).then_inc(lo_used.sem, 1)
                for j in range(PAIRS):
                    cs = th[:, j, :].rearrange("p (c t) -> p c t", t=CHUNK)
                    act.wait_ge(cum.sem, cum.at(5 * j + 5))
                    act.activation(EP[:, j, :, off:off + CHUNK], cs, ACT.Exp, scale=-DECAY).then_inc(ends.sem, 1)
                    if j >= 2:
                        act.wait_ge(done.sem, done.at(2 * (j - 1)))
                    act.activation(en[:, j % 2, :], th[:, j, :], ACT.Exp, scale=DECAY).then_inc(ends.sem, 1)
                    if ada:
                        self.ada_take(act, j)
                if ada:
                    self.ada_take(act, ADA_GROUPS - 1)

            @block.gpsimd
            def _(pool):
                pool.memset(lora[others], 0.0).then_inc(ones_col.sem, 1)
                pool.wait_ge(ones_col.sem, ones_col.at(1))
                pool.memset(EP[:, :, :, unit:unit + 1], 1.0).then_inc(ones_col.sem, 1)
                pool.wait_ge(ones_col.sem, ones_col.at(2))

            @block.vector
            def _(dve):
                o = Order(dve, order)
                for j in range(PAIRS):
                    dve.wait_ge(lo_used.sem, lo_used.at(6 * j + 3))
                    o.link(dve.tensor_scalar(th[:, j, :], th[:, j, :], 1.0, None, ALU.add))
                    run = th[:, j, :] if way == 0 else th[:, j, ::-1]
                    for q in range(T // 256):
                        part = run[:, q * 256:(q + 1) * 256]
                        dve.tensor_tensor_scan(out=part, data0=self.c("reset", 256), data1=part, initial=0.0,
                                               op0=ALU.mult, op1=ALU.add).then_inc(cum.sem, 1)
                for j in range(PAIRS):
                    dve.wait_ge(lo_used.sem, lo_used.at(6 * j + 6))
                    o(dve.scalar_tensor_tensor(out=Bs[:, j, :], in0=ta[:, j, :], scalar=1.0, in1=kk[:, j, :],
                                               op0=ALU.add, op1=ALU.mult))
                    o.wait()
                    o.link(dve.tensor_scalar(ta[:, j, :], ta[:, j, :], -1.0, self.dv(layer, "hk_a", 1, j),
                                             ALU.add, ALU.mult))
                    o.link(dve.scalar_tensor_tensor(out=Ks[:, j, :], in0=ta[:, j, :], scalar=1.0,
                                                    in1=tiles[:, T_RK + j, :], op0=ALU.add, op1=ALU.mult))
                    dve.wait_ge(ends.sem, ends.at(2 * j + 2))
                    dve.scalar_tensor_tensor(out=Bs[:, j, :], in0=Bs[:, j, :], scalar=0.5, in1=en[:, j % 2, :],
                                             op0=ALU.mult, op1=ALU.mult).then_inc(done.sem, 1)
                    dve.tensor_tensor(Ks[:, j, :], Ks[:, j, :], en[:, j % 2, :], ALU.mult).then_inc(done.sem, 1)
                if ada:
                    self.ada_finish(dve)
                self.total_order = o.n
        if ada:
            self.ada_close()
        order.close(self.total_order)
        lora_in.close(16), lo_in.close(18), lo_used.close(18), cum.close(15), ends.close(6), ones_col.close(2), done.close(6)

    def scan(self, layer, way):
        nc, d, tiles, bank = self.nc, self.d, self.tiles, self.bank
        names = ("prep", "turned", "turned_out", "amat", "nt_out", "arb_out", "k_raw", "k_diag", "joins", "x_start", "x_out",
                 "xt_out", "xt_last", "w_ready", "w_out", "xx_ready", "xx_out", "u0", "u0_out", "wu", "wu_out",
                 "ghr", "g_out", "h_out", "r_out", "yi", "yi_out", "yi_sum", "state", "state_out", "yo_out")
        prep, trs, tr_out, amat, nt_out, arb_out, k_raw, k_diag, joins, x0, x_out, xt_out, xt_last, w_rdy, w_out, xx_rdy, \
            xx_out, u0, u0_out, wu, wu_out, gr, g_out, h_out, r_out, yi, yi_out, yi_sum, st, st_out, yo_out = (
                self.sig(n) for n in names)
        v_in = [self.sig(f"v_in{s}") for s in range(2)]
        spaces = [[self.hid, 0, 6400], [self.tiles[:, 11:16, :].rearrange("p n t -> p (n t)"), 0, 6400],
                  [self.extra, 15480, 17408], [self.extra, 17472, self.NEX]]

        def take(n):
            for s in spaces:
                if s[1] + n <= s[2]:
                    s[1] += n
                    return s[0][:, s[1] - n:s[1]]
            raise ValueError("no room")
        jct = dict(j=PAIRS, c=2)
        def take_square():
            return take(RW).rearrange("p (q j t) -> p q j t", q=2, j=PAIRS)
        ntl = [take_square() for _ in range(2)]
        nt, xs, xt, wb, akk, ark, arb = (take_square() for _ in range(7))
        xtd = take(2 * RW).rearrange("p (q j c t) -> p q j c t", q=2, j=PAIRS, c=2)
        kkr = [take(2 * RW).rearrange("p (j s c t) -> p j s c t", s=2, **jct) for _ in range(2)]
        bch, kch, bend, kend, vs = ([take(RW) for _ in range(2)] for _ in range(5))
        pend = [take(2 * PAIRS).rearrange("p (j c) -> p j c", j=PAIRS) for _ in range(2)]
        rhs = take(2 * RW).rearrange("p (h s v) -> p h s v", h=HEADS, s=2)
        nbt, kt_ = take(RW), take(RW)
        wus = take(2 * RW).rearrange("p (h s v) -> p h s v", h=HEADS, s=2)
        raw = wus.rearrange("p h s v -> p (h s v)").rearrange("p (q n) -> p q n", q=2)
        gs, hs, rt = ([take(RW // 2).rearrange("p (j t) -> p j t", j=PAIRS) for _ in range(2)] for _ in range(3))
        yis = take(RW).rearrange("p (h v) -> p h v", h=HEADS)
        state = take(RW // 2).rearrange("p (j v) -> p j v", j=PAIRS)
        yacc = self.yacc = self.hid[:, 6400:6400 + NT * RW].rearrange("p (n h v) -> p n h v", n=NT, h=HEADS)
        EP, Bs, Ks, kk = self.EP, self.Bs, self.Ks, self.kk
        excl, incl, last = (0, 1, CHUNK) if way == 0 else (1, 0, 0)
        order_c = (0, 1) if way == 0 else (1, 0)
        half = [slice(HD * x, HD * x + HD) for x in range(2)]
        heads = [(j, p) for p in range(2) for j in range(PAIRS)]
        id64 = self.c("id64", HD)
        NL = len(LEVELS)

        def over_pairs(x):
            return x.unsqueeze(1).to_broadcast([P, PAIRS, x.shape[1]])

        def run(engine, body):
            for s in range(2):
                body(s, 0, s, s if way == 0 else 1 - s, True)
            with self.loop(engine, 1, NT // 2) as i:
                taus = [2 * i + s if way == 0 else i * -2 + (NT + 1 - s) for s in range(2)]
                for s in range(2):
                    body(s, i, 2 * i + s, taus[s], False)

        def bank3(i):
            return bank[i][:, 0:RW // 2].rearrange("p (j t) -> p j t", j=PAIRS)

        with nc.Block() as block:
            @block.sync
            def _(sp):
                def body(s, i, u, tau, first):
                    if not first:
                        sp.wait_ge(yo_out.sem, 2 * (u - 1) + yo_out.base)
                    sp.dma_start(vs[s], d["v_rw"][bass.ds(tau, 1)].rearrange("a p v -> (a p) v")).then_inc(v_in[s].sem, 16)
                run(ENGINE.SP, body)

            @block.gpsimd
            def _(pool):
                def body(s, i, u, tau, first):
                    def chunks(x):
                        return x.rearrange("p j (c t) -> p j c t", t=CHUNK)[:, :, bass.ds(2 * tau, 2), :]

                    def own(x):
                        return x.rearrange("p (j c t) -> p j c t", t=CHUNK, **jct)
                    if not first:
                        pool.wait_ge(yo_out.sem, 2 * (u - 1) + yo_out.base)
                    ep = EP[:, :, bass.ds(2 * tau, 2), :]
                    pend_b = ep[:, :, :, last:last + 1].to_broadcast([P, PAIRS, 2, CHUNK])
                    for ins in (
                        pool.tensor_tensor(kkr[s][:, :, 0], chunks(kk), ep[:, :, :, excl:excl + CHUNK], ALU.mult),
                        pool.tensor_tensor(own(bend[s]), chunks(Bs), pend_b, ALU.mult),
                        pool.tensor_tensor(own(kend[s]), chunks(Ks), pend_b, ALU.mult),
                        pool.tensor_tensor(kkr[s][:, :, 1], chunks(tiles[:, T_R:T_R + PAIRS, :]),
                                           ep[:, :, :, incl:incl + CHUNK], ALU.mult),
                        pool.tensor_copy(own(bch[s]), chunks(Bs)),
                        pool.tensor_copy(own(kch[s]), chunks(Ks)),
                        pool.tensor_copy(pend[s].unsqueeze(3), ep[:, :, :, last:last + 1]),
                    ):
                        ins.then_inc(prep.sem, 1)
                    def join(l):
                        mask = self.c("join", 5 * HD)[:, l * HD:(l + 1) * HD]
                        for q in range(2):
                            if l == 0:
                                pool.wait_ge(nt_out.sem, 2 * u + q + 1 + nt_out.base)
                            if l >= 2:
                                pool.wait_ge(w_rdy.sem, 2 * NL * u + 2 * (l - 2) + q + 1 + w_rdy.base)
                            masked(ntl[l % 2][:, q], nt[:, q], mask).then_inc(joins.sem, 1)

                    def masked(out, x, mask):
                        return pool.tensor_tensor(out, x, over_pairs(mask), ALU.mult)
                    join(0)
                    join(1)
                    for n, (dst, mask) in enumerate(((akk, f"akk{way}"), (ark, f"ark{way}"))):
                        for q in range(2):
                            if n == 0:
                                pool.wait_ge(k_raw.sem, 2 * u + q + 1 + k_raw.base)
                            x = raw[:, q].rearrange("p (j s t) -> p j s t", j=PAIRS, s=2)[:, :, n, :]
                            masked(dst[:, q], x, self.c(mask, HD)).then_inc(k_diag.sem, 1)
                    for l in range(2, NL):
                        join(l)
                    if way:
                        pool.wait_ge(yi_out.sem, u + 1 + yi_out.base)
                        pool.tensor_tensor(yis, yis, yacc[:, bass.ds(tau, 1)].rearrange("p a h v -> p (a h) v"),
                                           ALU.add).then_inc(yi_sum.sem, 1)
                run(ENGINE.Pool, body)

            @block.tensor
            def _(pe):
                def body(s, i, u, tau, first):
                    again = not (first and s == 0)

                    def hold(x, per_unit, more):
                        count = per_unit * u + more + x.base
                        if not first:
                            count = pe.to_reg(count)
                            pe.wait_ge(x.sem, x.at(2 * per_unit + more))
                        pe.wait_ge(x.sem, count)
                    hold(prep, 7, 3)
                    if again:
                        hold(yo_out, 2, 0)
                        hold(st_out, 2, 1)
                    for m, src in enumerate((None, bend[s], kend[s])):
                        for j in range(PAIRS):
                            x = kkr[s][:, j, 0].rearrange("p c t -> p (c t)") if m == 0 else src[:, j * P:(j + 1) * P]
                            ins = pe.transpose(bank[m][:, j * P:(j + 1) * P], x, self.c("ident", P))
                        ins.then_inc(trs.sem, 1)
                    hold(prep, 7, 6)
                    for b0, left in ((3, bch[s]), (5, kch[s])):
                        for p in range(2):
                            for j in range(PAIRS):
                                for c in range(2):
                                    ins = pe.matmul(bank[b0 + p][half[c], j * P:(j + 1) * P],
                                                    left[half[p], (2 * j + c) * HD:(2 * j + c + 1) * HD],
                                                    kkr[s][half[p], j, :, c, :], start=True, stop=True)
                            ins.then_inc(amat.sem, 1)
                    hold(tr_out, 3, 3)
                    for l in range(NL):
                        for p in range(2):
                            if l == 0:
                                hold(x_out, 2, p + 1)
                            else:
                                hold(xx_out, 2 * NL - 2, 2 * (l - 1) + p + 1)
                            hold(joins, 2 * NL, 2 * l + p + 1)
                            for j in range(PAIRS):
                                for c in range(2):
                                    ins = pe.matmul(bank[1 + p][half[c], j * HD:(j + 1) * HD],
                                                    ntl[l % 2][half[c], p, j, :], xs[half[c], p, j, :],
                                                    start=True, stop=True)
                            ins.then_inc(w_rdy.sem, 1)
                        for p in range(2):
                            hold(w_out, 2 * NL, 2 * l + p + 1)
                            hold(xt_out, 2 * NL, 2 * l + p + 1)
                            left, right = (xt, wb) if l < NL - 1 else (wb, xt)
                            for j in range(PAIRS):
                                for c in range(2):
                                    ins = pe.matmul(bank[3 + p][half[c], j * HD:(j + 1) * HD], left[half[c], p, j, :],
                                                    right[half[c], p, j, :], start=True, stop=True)
                            ins.then_inc(xx_rdy.sem, 1)
                        if l == 1:
                            hold(v_in[s], 8, 16 - 8 * s)
                            hold(k_diag, 4, 2)
                            for j, p in heads:
                                for c in range(2):
                                    hc = slice((2 * j + p) * HD, (2 * j + p + 1) * HD)
                                    ins = pe.matmul(bank[5][half[c], hc], akk[half[c], p, j, :], vs[s][half[c], hc],
                                                    start=True, stop=True)
                            ins.then_inc(u0.sem, 1)
                    hold(u0_out, 1, 1)
                    for p in range(2):
                        hold(xt_last, 4, 2 * p + 2)
                        for j in range(PAIRS):
                            ins = pe.matmul(bank[6 + p][:, j * P:(j + 1) * P],
                                            xtd[:, p, j].rearrange("p c t -> p (c t)"),
                                            rhs[:, 2 * j + p].rearrange("p s v -> p (s v)"), start=True, stop=True)
                        ins.then_inc(wu.sem, 1)
                    hold(wu_out, 2, 2)
                    for c in order_c:
                        for j, p in heads:
                            h = 2 * j + p
                            ins = pe.matmul(bank[c][half[p], j * HD:(j + 1) * HD], wus[half[c], h, 0, :],
                                            nbt[half[c], h * HD:(h + 1) * HD], start=True, stop=True)
                        ins.then_inc(gr.sem, 1)
                        for j, p in heads:
                            h = 2 * j + p
                            hc = slice(h * HD, (h + 1) * HD)
                            pe.matmul(bank[2 + c][half[p], j * HD:(j + 1) * HD], kt_[half[c], hc], vs[s][half[c], hc],
                                      start=True, stop=False)
                            ins = pe.matmul(bank[2 + c][half[p], j * HD:(j + 1) * HD], nbt[half[c], hc],
                                            wus[half[c], h, 1, :], start=False, stop=True)
                        ins.then_inc(gr.sem, 1)
                        for j, p in heads:
                            ins = pe.matmul(bank[4 + c][half[p], j * HD:(j + 1) * HD], wus[half[c], 2 * j + p, 0, :],
                                            arb[half[c], p, j, :], start=True, stop=True)
                        ins.then_inc(gr.sem, 1)
                    hold(k_diag, 4, 4)
                    for j, p in heads:
                        h = 2 * j + p
                        hc = slice(h * HD, (h + 1) * HD)
                        for c in range(2):
                            pe.matmul(bank[6][half[c], hc], ark[half[c], p, j, :], vs[s][half[c], hc],
                                      start=True, stop=False)
                            ins = pe.matmul(bank[6][half[c], hc], arb[half[c], p, j, :], wus[half[c], h, 1, :],
                                            start=False, stop=True)
                    ins.then_inc(yi.sem, 1)
                    hold(g_out, 6, 6)
                    hold(h_out, 2, 2)
                    hold(r_out, 2, 2)
                    for m, c in enumerate(order_c):
                        hold(st_out, 2, m + 1)
                        for j, p in heads:
                            ins = pe.matmul(bank[1 + m][half[p], j * HD:(j + 1) * HD], gs[c][half[p], j, :],
                                            state[half[p], j, :], start=True, stop=True)
                        for j, p in heads:
                            ins = pe.matmul(bank[7 - 7 * p][half[c], j * HD:(j + 1) * HD], rt[c][half[p], j, :],
                                            state[half[p], j, :], start=True, stop=True)
                        ins.then_inc(st.sem, 1)
                run(ENGINE.PE, body)

            @block.scalar
            def _(act):
                def body(s, i, u, tau, first):
                    for m, (dst, scale) in enumerate(((rhs[:, :, 0, :], 1.0), (nbt, -1.0), (kt_, 1.0))):
                        act.wait_ge(trs.sem, 3 * u + m + 1 + trs.base)
                        src = bank[m][:, 0:RW]
                        if m == 0:
                            src = src.rearrange("p (h v) -> p h v", h=HEADS)
                        act.activation(dst, src, ACT.Copy, scale=scale).then_inc(tr_out.sem, 1)
                    for p in range(2):
                        act.wait_ge(amat.sem, 4 * u + p + 3 + amat.base)
                        act.copy(raw[:, p], bank[5 + p][:, 0:RW]).then_inc(k_raw.sem, 1)
                    for l in range(NL):
                        for p in range(2):
                            act.wait_ge(xx_rdy.sem, 2 * NL * u + 2 * l + p + 1 + xx_rdy.base)
                            if l < NL - 1:
                                act.copy(xs[:, p], bank3(3 + p)).then_inc(xx_out.sem, 1)
                            else:
                                for c in range(2):
                                    act.copy(xtd[half[c], p, :, c, :], bank3(3 + p)[half[c]]).then_inc(xt_last.sem, 1)
                    act.wait_ge(k_diag.sem, 4 * u + 4 + k_diag.base)
                    for p in range(2):
                        act.wait_ge(wu.sem, 2 * u + p + 1 + wu.base)
                        act.copy(wus.rearrange("p (j q) s v -> p j q (s v)", q=2)[:, :, p, :],
                                 bank[6 + p][:, 0:RW].rearrange("p (j x) -> p j x", j=PAIRS)).then_inc(wu_out.sem, 1)
                    for m, c in enumerate(order_c):
                        act.wait_ge(gr.sem, 6 * u + 3 * m + 2 + gr.base)
                        act.copy(hs[c], bank3(2 + c)).then_inc(h_out.sem, 1)
                    act.wait_ge(yi.sem, u + 1 + yi.base)
                    if not (first and s == 0):
                        act.wait_ge(yo_out.sem, 2 * u + yo_out.base)
                    act.copy(yis, bank[6][:, 0:RW].rearrange("p (h v) -> p h v", h=HEADS)).then_inc(yi_out.sem, 1)
                run(ENGINE.Activation, body)

            @block.vector
            def _(dve):
                dve.memset(xtd, 0.0)
                dve.memset(state, 0.0).then_inc(st_out.sem, 1)

                def body(s, i, u, tau, first):
                    for p in range(2):
                        dve.wait_ge(amat.sem, 4 * u + p + 1 + amat.base)
                        x = bank[3 + p][:, 0:RW].rearrange("p (j s t) -> p j s t", j=PAIRS, s=2)
                        dve.tensor_tensor(nt[:, p], x[:, :, 0, :], over_pairs(self.c(f"strict{way}", HD)),
                                          ALU.mult).then_inc(nt_out.sem, 1)
                        dve.tensor_tensor(arb[:, p], x[:, :, 1, :], over_pairs(self.c(f"arb{way}", HD)),
                                          ALU.mult).then_inc(arb_out.sem, 1)
                    for p in range(2):
                        dve.wait_ge(nt_out.sem, 2 * u + p + 1 + nt_out.base)
                        dve.tensor_tensor(xt[:, p], nt[:, p], over_pairs(self.c(f"first{way}", HD)),
                                          ALU.mult).then_inc(x0.sem, 1)
                    for p in range(2):
                        dve.wait_ge(x0.sem, 2 * u + p + 1 + x0.base)
                        dve.tensor_tensor(xt[:, p], xt[:, p], over_pairs(id64), ALU.add).then_inc(xt_out.sem, 1)

                    def turn(out, x):
                        return dve.transpose(out, x)
                    for p in range(2):
                        dve.wait_ge(xt_out.sem, 2 * NL * u + p + 1 + xt_out.base)
                        turn(xs[:, p], xt[:, p]).then_inc(x_out.sem, 1)
                    for l in range(NL):
                        for p in range(2):
                            dve.wait_ge(w_rdy.sem, 2 * NL * u + 2 * l + p + 1 + w_rdy.base)
                            dve.tensor_tensor(wb[:, p], bank3(1 + p), over_pairs(id64), ALU.add).then_inc(w_out.sem, 1)
                        if l < NL - 1:
                            for p in range(2):
                                dve.wait_ge(xx_out.sem, (2 * NL - 2) * u + 2 * l + p + 1 + xx_out.base)
                                turn(xt[:, p], xs[:, p]).then_inc(xt_out.sem, 1)
                        if l == 1:
                            dve.wait_ge(u0.sem, u + 1 + u0.base)
                            dve.tensor_copy(rhs[:, :, 1, :], bank[5][:, 0:RW].rearrange("p (h v) -> p h v", h=HEADS)
                                            ).then_inc(u0_out.sem, 1)
                    dve.wait_ge(prep.sem, 7 * u + 7 + prep.base)
                    for m, c in enumerate(order_c):
                        dve.wait_ge(gr.sem, 6 * u + 3 * m + 1 + gr.base)
                        for j in range(PAIRS):
                            dve.scalar_tensor_tensor(out=gs[c][:, j, :], in0=id64, scalar=pend[s][:, j, c:c + 1],
                                                     in1=bank3(c)[:, j, :], op0=ALU.mult, op1=ALU.add
                                                     ).then_inc(g_out.sem, 1)
                        dve.wait_ge(gr.sem, 6 * u + 3 * m + 3 + gr.base)
                        dve.tensor_tensor(rt[c], bank3(4 + c), kkr[s][:, :, 1, c, :], ALU.add).then_inc(r_out.sem, 1)
                    for m, c in enumerate(order_c):
                        dve.wait_ge(st.sem, 2 * u + m + 1 + st.base)
                        dve.wait_ge(h_out.sem, 2 * u + m + 1 + h_out.base)
                        dve.tensor_tensor(state, bank3(1 + m), hs[c], ALU.add).then_inc(st_out.sem, 1)
                    if way:
                        dve.wait_ge(yi_sum.sem, u + 1 + yi_sum.base)
                    else:
                        dve.wait_ge(yi_out.sem, u + 1 + yi_out.base)
                    part = yacc[:, bass.ds(tau, 1)].rearrange("p a (j q) v -> p (a j) q v", q=2)
                    for p in range(2):
                        dve.tensor_tensor(part[:, :, p, :], bank3(7 - 7 * p),
                                          yis.rearrange("p (j q) v -> p j q v", q=2)[:, :, p, :],
                                          ALU.add).then_inc(yo_out.sem, 1)
                run(ENGINE.DVE, body)
        n = NT
        for x, k in ((v_in[0], 8), (v_in[1], 8), (prep, 7), (trs, 3), (tr_out, 3), (amat, 4), (nt_out, 2), (arb_out, 2),
                     (k_raw, 2), (k_diag, 4), (joins, 2 * NL), (x0, 2), (x_out, 2), (xt_out, 2 * NL), (xt_last, 4),
                     (w_rdy, 2 * NL), (w_out, 2 * NL), (xx_rdy, 2 * NL), (xx_out, 2 * NL - 2), (u0, 1), (u0_out, 1),
                     (wu, 2), (wu_out, 2), (gr, 6), (g_out, 6), (h_out, 2), (r_out, 2), (yi, 1), (yi_out, 1),
                     (yi_sum, way), (st, 2), (yo_out, 2)):
            x.close(k * n)
        st_out.close(2 * n + 1)

    def readout(self, layer):
        nc, d, tiles = self.nc, self.d, self.tiles
        keep = layer < DEPTH - 1
        n0 = 0 if keep else CTX // P
        cnt = NT - n0
        back, order, act_order, var_ready, y_ready, turned, done = (self.sig(n) for n in (
            "read_in", "order_dve", "var_root", "var_ready", "y_ready", "y_turned", "y_gated"))
        y = self.yacc[:, n0:, :, :].rearrange("p n h v -> p (n h) v")
        G = cnt * HEADS
        tmp = self.hid[:, 0:G * HD].rearrange("p (g v) -> p g v", v=HD)
        v = self.ex(0, G * HD).rearrange("p (g v) -> p g v", v=HD)
        ln = self.ex(3840, 2 * RW).rearrange("p (s v) -> p s v", s=2)
        mean = self.ex(3840 + 768, G)
        var = self.ex(3840 + 768 + 64, G)
        bonus = self.bonus[:, n0:, :].rearrange("p n h -> p (n h)")

        def bc(x):
            return x.unsqueeze(2).to_broadcast([P, G, HD])

        def row(s):
            return ln[:, s:s + 1, :].to_broadcast([P, cnt, RW])
        flat = y.rearrange("p (n h) v -> p n (h v)", h=HEADS)
        with nc.Block() as block:
            @block.sync
            def _(sp):
                lo = n0 * P
                sp.dma_start(ln, d["ln"][layer]).then_inc(back.sem, 16)
                sp.dma_start(v.rearrange("p (n h) v -> p n (h v)", h=HEADS),
                             d["v_rw"][n0:].rearrange("n p v -> p n v")).then_inc(back.sem, 16)
                sp.dma_start(tiles[:, 11:16, lo:T], d["y"].rearrange("n p t -> p n t")[:, :, lo:T]).then_inc(back.sem, 16)
                xsrc = d["x"] if layer == 0 else d["x_mid"]
                sp.dma_start(tiles[:, 0:KT, lo:T], xsrc[:, :, lo:T]).then_inc(back.sem, 16)
                sp.wait_ge(back.sem, back.at(64))

            @block.vector
            def _(dve):
                o = Order(dve, order)
                o.link(dve.reduce_sum(mean, y, AX.X))
                o.link(dve.tensor_scalar(mean, mean, 1.0 / HD, None, ALU.mult))
                o.link(dve.tensor_tensor(y, y, bc(mean), ALU.subtract))
                o.link(dve.tensor_tensor(tmp, y, y, ALU.mult))
                dve.reduce_sum(var, tmp, AX.X).then_inc(var_ready.sem, 1)
                dve.wait_ge(act_order.sem, act_order.at(1))
                o.link(dve.reciprocal(var, var))
                o.link(dve.tensor_tensor(y, y, bc(var), ALU.mult))
                dve.wait_ge(back.sem, back.at(64))
                o.link(dve.tensor_tensor(flat, flat, row(0), ALU.mult))
                o.link(dve.tensor_tensor(flat, flat, row(1), ALU.add))
                o.link(dve.tensor_tensor(tmp, v, bc(bonus), ALU.mult))
                dve.tensor_tensor(y, y, tmp, ALU.add).then_inc(y_ready.sem, 1)
                for n in range(n0, NT):
                    dve.wait_ge(turned.sem, turned.at(n - n0 + 1))
                    gate = tiles[:, T_G:T_G + PAIRS, n * P:(n + 1) * P]
                    dve.tensor_tensor(gate, self.bank[n % 2][:, 0:RW].rearrange("p (j t) -> p j t", j=PAIRS), gate,
                                      ALU.mult).then_inc(done.sem, 1)
                self.total_order = o.n

            @block.scalar
            def _(act):
                act.wait_ge(var_ready.sem, var_ready.at(1))
                act.activation(var, var, ACT.Sqrt, scale=1.0 / HD, bias=self.eps[:, 1:2]).then_inc(act_order.sem, 1)

            @block.tensor
            def _(pe):
                pe.wait_ge(y_ready.sem, y_ready.at(1))
                for n in range(n0, NT):
                    if n - n0 >= 2:
                        pe.wait_ge(done.sem, done.at(n - n0 - 1))
                    for j in range(PAIRS):
                        ins = pe.transpose(self.bank[n % 2][:, j * P:(j + 1) * P], flat[:, n - n0, j * P:(j + 1) * P],
                                           self.c("ident", P))
                    ins.then_inc(turned.sem, 1)
        order.close(self.total_order)
        back.close(64), act_order.close(1), var_ready.close(1), y_ready.close(1), turned.close(cnt), done.close(cnt)

    def project_out(self, layer):
        nc, d, tiles = self.nc, self.d, self.tiles
        keep = layer < DEPTH - 1
        groups = GROUPS if keep else GROUPS[1:]
        ng = len(groups)
        ready, free, x_out = (self.sig(n) for n in ("acc_ready", "acc_free", "dma_out"))
        taken = self.sig("res_free")
        ring = [self.ex(s * DM, DM).rearrange("p (k n) -> p k n", k=KT) for s in range(2)]
        with nc.Block() as block:
            @block.sync
            def _(sp):
                self.stream_sync(sp, d["w_out"][layer], KT, ring, ng)
                if keep:
                    sp.wait_ge(taken.sem, taken.at(ng * KT))
                    sp.dma_start(d["x_mid"], tiles[:, 0:KT, :]).then_inc(x_out.sem, 16)
                    sp.wait_ge(x_out.sem, x_out.at(16))

            @block.tensor
            def _(pe):
                save, self.signals["acc_free"] = self.signals["acc_free"], taken
                self.stream_pe(pe, tiles[:, KT:2 * KT, :], KT, ring, groups, groups)
                self.signals["acc_free"] = save

            @block.vector
            def _(dve):
                with self.loop(ENGINE.DVE, 0, KT // 2) as i:
                    for s in range(2):
                        t = 2 * i + s
                        for q, (a, b) in enumerate(groups):
                            gate = self.ada[:, layer, bass.ds(2 * KT + t, 1), (1 if a == 0 else 0)]
                            x = tiles[:, bass.ds(t, 1), a:b].rearrange("p n t -> p (n t)")
                            dve.wait_ge(ready.sem, ng * t + q + 1 + ready.base)
                            dve.scalar_tensor_tensor(out=x, in0=self.bank[3 * s + q][:, 0:b - a], scalar=gate,
                                                     in1=x, op0=ALU.mult, op1=ALU.add).then_inc(taken.sem, 1)
        self.sig("w_in0").close(8 * KT), self.sig("w_in1").close(8 * KT), ready.close(ng * KT), taken.close(ng * KT)
        x_out.close(16 if keep else 0)

    def final_norm(self):
        nc, d = self.nc, self.d
        sq = self.ex(0, 4 * T).rearrange("p (s t) -> p s t", s=4)
        rstd = self.ex(4 * T, T)
        x = self.tiles[:, 0:KT, :]
        roots, order, outs, stored = (self.sig(n) for n in ("roots", "order_dve", "outs", "dma_out"))
        groups = GROUPS[1:]
        with nc.Block() as block:
            add_pairs = self.inv_rms(block, x, sq, rstd, CTX, groups)

            @block.vector
            def _(dve):
                o = Order(dve, order)
                add_pairs(dve)
                for n, (a, b) in enumerate(groups):
                    dve.wait_ge(roots.sem, roots.at(n + 1))
                    o(dve.reciprocal(rstd[:, a:b], rstd[:, a:b]))
                o.wait()
                for k in range(KT):
                    dve.scalar_tensor_tensor(out=x[:, k, CTX:T], in0=x[:, k, CTX:T], scalar=self.fing[:, k:k + 1],
                                             in1=rstd[:, CTX:T], op0=ALU.mult, op1=ALU.mult).then_inc(outs.sem, 1)

            @block.sync
            def _(sp):
                for k in range(KT):
                    sp.wait_ge(outs.sem, outs.at(k + 1))
                    sp.dma_start(d["out"][:, k, :], x[:, k, CTX:T]).then_inc(stored.sem, 16)
                sp.wait_ge(stored.sem, stored.at(16 * KT))


def column_order():
    sizes = (384, 384, 384, 384, 128, 128, 384, 128, 128, 384, 256, 256, 256, 256)
    starts = np.concatenate([[0], np.cumsum(sizes)[:-1]])
    r, k, v, g, wd, ad, q, ka, va, ga, bg, cg, xin, cgate = (
        np.arange(s, s + n) for s, n in zip(starts, sizes))
    first = np.concatenate([cg, xin, bg, cgate, q[head_order()], ga[head_order()], ka])
    second = np.concatenate([r, k, wd, ad, g])
    return first, second, np.concatenate([v, va])


def head_order():
    return np.concatenate([np.arange(HD) + HD * h for j in range(PAIRS) for h in (j, PAIRS + j)])


def const_table():
    out = np.zeros((P, NCONST), np.float32)

    def put(name, x):
        out[:, CONST[name]:CONST[name] + x.shape[1]] = x
    i = np.arange(P)
    put("ident", np.eye(P))
    rot = np.zeros((P, P))
    for h in (0, HD):
        for m in range(HD // 2):
            rot[h + m + HD // 2, h + m] = -1
            rot[h + m, h + m + HD // 2] = 1
    put("rot", rot)
    put("headsum", (i[:, None] // HD == i[None, :] // HD))
    put("ones", np.ones((P, P)))
    put("headsel", i[:, None] // HD == np.arange(2)[None, :])
    put("reset", np.broadcast_to(np.arange(256) % CHUNK != 0, (P, 256)))
    a, b = i[:, None] % HD, np.arange(HD)[None, :]
    put("id64", a == b)
    join = [(a // (2 * m) == b // (2 * m)) & (a // m != b // m) for m in (1,) + LEVELS]
    put("join", np.concatenate(join[1:], 1))
    for way, after in enumerate((b > a, b < a)):
        put(f"strict{way}", -after.astype(np.float32))
        put(f"arb{way}", -(after | (a == b)).astype(np.float32))
        put(f"akk{way}", after)
        put(f"ark{way}", after | (a == b))
        put(f"first{way}", after & join[0])
    return out


def trig_table():
    inv = np.float32(10000.0) ** (-np.arange(HD // 4, dtype=np.float32) / np.float32(HD // 4))
    t = np.arange(SEQ)
    ang = np.concatenate([(t // 64).astype(np.float32)[:, None] * inv, (t % 64).astype(np.float32)[:, None] * inv], 1)
    freq = np.arange(P) % (HD // 2)
    return np.stack([np.cos(ang).T[freq], np.sin(ang).T[freq]], 1).astype(np.float32)


def strip_table():
    out = np.zeros((P, 2, QB, P), np.float32)
    q, k = np.arange(P)[:, None], np.arange(P)[None, :]
    out[:, 0] = np.where(k >= q, 0.0, MASK_VALUE)[:, None]
    out[:, 1] = np.where(k <= q, 0.0, MASK_VALUE)[:, None]
    out[:, 0, 0] = MASK_VALUE
    out[:, 1, QB - 1] = MASK_VALUE
    return out.reshape(P, 2, QB * P)


def kernel(x, c, ctx, c_ctx, w_ada, b_ada, norm_g, w_in, w_out, rw_w0, rw_w_up, rw_a0, rw_a_up, rw_k_k, rw_k_a,
           rw_r_k, rw_ln_g, rw_ln_b, at_sink, cv_w, final_g):
    import concourse.bacc as bacc
    from concourse.bass_utils import run_bass_kernel_spmd

    def channels(a):
        a = np.asarray(a)
        return np.moveaxis(a.reshape(a.shape[:-1] + (-1, P)), -1, 0)

    def weight_tiles(w, n):
        w = np.asarray(w)
        return w.reshape(DEPTH, KT, P, -1, n).transpose(0, 3, 2, 1, 4)
    first, second, values = column_order()
    w_in, w_out = np.asarray(w_in), np.asarray(w_out)
    rows = np.concatenate([np.arange(RW), RW + head_order(), np.arange(2 * RW, DM)])
    tokens = np.concatenate([np.asarray(ctx)[0], np.asarray(x)[0]], 0)
    param = np.concatenate([
        channels(norm_g), channels(rw_w0).reshape(P, DEPTH, -1), channels(rw_a0).reshape(P, DEPTH, -1),
        channels(rw_k_k), channels(rw_k_a), channels(np.asarray(rw_r_k).reshape(DEPTH, RW)),
        channels(cv_w).reshape(P, DEPTH, -1),
        np.broadcast_to(np.asarray(at_sink).reshape(DEPTH, 2, PAIRS).transpose(0, 2, 1).reshape(1, DEPTH, HEADS),
                        (P, DEPTH, HEADS)),
        channels(b_ada)], -1)
    lora = np.stack([np.asarray(rw_w_up).reshape(DEPTH, P, RW), np.asarray(rw_a_up).reshape(DEPTH, P, RW)], 2)
    ln = np.broadcast_to(np.stack([np.asarray(rw_ln_g), np.asarray(rw_ln_b)], 1)[:, None], (DEPTH, P, 2, RW))
    cc = np.stack([np.asarray(c)[0].reshape(KT, P).T, np.asarray(c_ctx).reshape(KT, P).T], 2)
    arrays = {
        "x": np.moveaxis(tokens.T.reshape(KT, P, T), 0, 1), "cc": cc, "const": const_table(), "param": param,
        "fing": channels(final_g), "w_ada": weight_tiles(w_ada, 512).reshape(-1, P, KT, 512),
        "w_1": weight_tiles(w_in[:, :, first], P), "w_2": weight_tiles(w_in[:, :, second], P),
        "w_v": weight_tiles(w_in[:, :, values], 512)[:, 0], "w_out": weight_tiles(w_out[:, rows], P),
        "lora": lora, "ln": ln, "trig": trig_table(), "strips": strip_table(),
    }
    arrays = {k: np.ascontiguousarray(v) for k, v in arrays.items()}
    nc = bacc.Bacc("TRN2", target_bir_lowering=False, num_devices=1)
    d = {k: nc.dram_tensor(f"in_{k}", v.shape, F32, kind="ExternalInput").ap() for k, v in arrays.items()}
    d["out"] = nc.dram_tensor("out", (P, KT, SEQ), F32, kind="ExternalOutput").ap()
    for name, shape in (("v_rw", (NT, P, RW)), ("y", (5, P, T)), ("x_mid", (P, KT, T))):
        d[name] = nc.dram_tensor(name, shape, F32).ap()
    build(nc, d)
    r = run_bass_kernel_spmd(nc, [{f"in_{k}": v for k, v in arrays.items()}], core_ids=[0])
    out = r.results[0]["out"]
    return np.ascontiguousarray(np.moveaxis(out, 1, 0).reshape(DM, SEQ).T.reshape(1, SEQ, DM))
```
